# Optimizing a Trainium2 kernel written in Bass

```python
import math
import jax
import jax.numpy as jnp
from jax import lax
import numpy as np
import jax, jax.numpy as jnp

D_MODEL = 1024
BATCH = 1
SEQ = 1024
DEPTH = 1

CTX_LEN = 256
GRID_W = 64
ROPE_BASE = 10000.0
NORM_EPS = 1e-6

DA_HEADS = 4
DA_QK_DIM = 64
DA_V_DIM = 2 * DA_QK_DIM
DA_WIDTH = DA_HEADS * DA_V_DIM
Q_BLOCK = 128

GLA_HEADS = 4
GLA_K_DIM = 64
GLA_V_DIM = 128
GLA_WIDTH = GLA_HEADS * GLA_V_DIM
GLA_GATE_RANK = 16
GLA_GATE_TAU = 16.0
GLA_CHUNK = 64

MIX_WIDTH = DA_WIDTH + GLA_WIDTH
IN_PROJ_SIZES = (DA_HEADS * 2 * DA_QK_DIM, DA_HEADS * 2 * DA_QK_DIM, DA_WIDTH,
                 GLA_HEADS * GLA_K_DIM, GLA_HEADS * GLA_K_DIM, GLA_WIDTH, GLA_WIDTH,
                 GLA_GATE_RANK, GLA_GATE_RANK)
IN_PROJ_DIM = sum(IN_PROJ_SIZES)

N_GROUPS = 4
EXPERTS_PER_GROUP = 8
N_EXPERTS = N_GROUPS * EXPERTS_PER_GROUP
TOP_K = 2
EXPERT_HIDDEN = 512
DISPATCH_BLOCK = 128


def rms_norm(x, gain):
    xf = x.astype(jnp.float32)
    y = xf * lax.rsqrt(jnp.mean(xf * xf, axis=-1, keepdims=True) + NORM_EPS)
    return (y * gain.astype(jnp.float32)).astype(x.dtype)

def modulate(h, shift, scale):
    return h * (1 + scale) + shift

def split_in_proj(p):
    parts, start = [], 0
    for size in IN_PROJ_SIZES:
        parts.append(p[..., start:start + size])
        start += size
    return parts

def axial_rope_tables(rows, rot_dim):
    n_freq = rot_dim // 4
    r, col = jnp.meshgrid(jnp.arange(rows, dtype=jnp.float32),
                          jnp.arange(GRID_W, dtype=jnp.float32), indexing="ij")
    pos = jnp.stack([r.reshape(-1), col.reshape(-1)], axis=-1)
    inv_freq = jnp.power(ROPE_BASE, -jnp.arange(n_freq, dtype=jnp.float32) / n_freq)
    ang = pos[:, :, None] * inv_freq
    return jnp.cos(ang), jnp.sin(ang)

def apply_axial_rope(x, cos, sin):
    n_freq = cos.shape[-1]
    xr = x.reshape(x.shape[:-1] + (2, 2, n_freq))
    x1, x2 = xr[..., 0, :], xr[..., 1, :]
    cs, sn = cos.astype(x.dtype), sin.astype(x.dtype)
    out = jnp.stack([x1 * cs - x2 * sn, x2 * cs + x1 * sn], axis=-2)
    return out.reshape(x.shape)

def diff_attend(q, k, v, lam):
    s = jnp.einsum("bqhmd,bkhmd->bhmqk", q, k).astype(jnp.float32) * (DA_QK_DIM ** -0.5)
    p = jax.nn.softmax(s, axis=-1)
    a = p[:, :, 0] - lam * p[:, :, 1]
    return jnp.einsum("bhqk,bkhe->bqhe", a.astype(v.dtype), v)

def gla_chunked(q, k, v, log_a, s0):
    B, T, H, dk = q.shape
    dv = v.shape[-1]
    n_chunks = T // GLA_CHUNK

    def chunks(t):
        return jnp.moveaxis(t.reshape(B, n_chunks, GLA_CHUNK, H, t.shape[-1]), 1, 0)

    mask = jnp.tril(jnp.ones((GLA_CHUNK, GLA_CHUNK), dtype=bool))

    def step(state, inp):
        qi, ki, vi, gi = inp
        b = jnp.cumsum(gi.astype(jnp.float32), axis=1)
        b_last = b[:, -1]
        q_dec = qi * jnp.exp(b)
        k_inv = ki * jnp.exp(-b)
        scores = jnp.einsum("bihk,bjhk->bhij", q_dec, k_inv)
        scores = jnp.where(mask, scores, 0.0)
        o = (jnp.einsum("bhij,bjhv->bihv", scores, vi)
             + jnp.einsum("bihk,bhkv->bihv", q_dec, state))
        k_to_end = ki * jnp.exp(b_last[:, None] - b)
        new_state = (state * jnp.exp(b_last)[..., None]
                     + jnp.einsum("bjhk,bjhv->bhkv", k_to_end, vi))
        return new_state, o

    s_final, o = lax.scan(step, s0, (chunks(q), chunks(k), chunks(v), chunks(log_a)))
    o = jnp.moveaxis(o, 0, 1).reshape(B, T, H, dv)
    return o, s_final

def log_gate(lowrank, w2, b):
    return jax.nn.log_sigmoid((lowrank @ w2 + b).astype(jnp.float32)) / GLA_GATE_TAU

def token_mixer(h_lat, h_ctx, cos, sin, lambda_init, w_in, da_lambda, da_subln_g,
                gla_gate_w2, gla_gate_b, gla_norm_g, w_out, with_ctx_out):
    B, S, _ = h_lat.shape
    L = h_ctx.shape[1]
    dt = h_lat.dtype
    dq_l, dk_l, dv_l, gq_l, gk_l, gv_l, gr_l, lrf_l, lrb_l = split_in_proj(h_lat @ w_in)
    dq_c, dk_c, dv_c, gq_c, gk_c, gv_c, gr_c, lrf_c, lrb_c = split_in_proj(h_ctx @ w_in)

    cos_b, sin_b = cos[:, None, None], sin[:, None, None]
    q_l = apply_axial_rope(dq_l.reshape(B, S, DA_HEADS, 2, DA_QK_DIM), cos_b, sin_b)
    k_l = apply_axial_rope(dk_l.reshape(B, S, DA_HEADS, 2, DA_QK_DIM), cos_b, sin_b)
    v_l = dv_l.reshape(B, S, DA_HEADS, DA_V_DIM)
    k_c = dk_c.reshape(B, L, DA_HEADS, 2, DA_QK_DIM)
    v_c = dv_c.reshape(B, L, DA_HEADS, DA_V_DIM)
    lam_p = da_lambda.astype(jnp.float32)
    lam = (jnp.exp(jnp.sum(lam_p[0] * lam_p[1])) - jnp.exp(jnp.sum(lam_p[2] * lam_p[3]))
           + lambda_init)
    k_all = jnp.concatenate([k_c, k_l], axis=1)
    v_all = jnp.concatenate([v_c, v_l], axis=1)
    qb = jnp.moveaxis(q_l.reshape(B, S // Q_BLOCK, Q_BLOCK, DA_HEADS, 2, DA_QK_DIM), 1, 0)
    a_l = lax.map(lambda qi: diff_attend(qi, k_all, v_all, lam), qb)
    a_l = jnp.moveaxis(a_l, 0, 1).reshape(B, S, DA_HEADS, DA_V_DIM)
    a_l = rms_norm(a_l, da_subln_g) * (1.0 - lambda_init)

    def gla_inputs(gq, gk, gv, lrf, lrb, n):
        q = gq.reshape(B, n, GLA_HEADS, GLA_K_DIM) * (GLA_K_DIM ** -0.5)
        k = gk.reshape(B, n, GLA_HEADS, GLA_K_DIM)
        v = gv.reshape(B, n, GLA_HEADS, GLA_V_DIM)
        g_f = log_gate(lrf, gla_gate_w2[0], gla_gate_b[0]).reshape(B, n, GLA_HEADS, GLA_K_DIM)
        g_b = log_gate(lrb, gla_gate_w2[1], gla_gate_b[1]).reshape(B, n, GLA_HEADS, GLA_K_DIM)
        return q, k, v, g_f, g_b

    gql, gkl, gvl, gfl, gbl = gla_inputs(gq_l, gk_l, gv_l, lrf_l, lrb_l, S)
    gqc, gkc, gvc, gfc, gbc = gla_inputs(gq_c, gk_c, gv_c, lrf_c, lrb_c, L)
    flip = lambda t: jnp.flip(t, axis=1)
    s0 = jnp.zeros((B, GLA_HEADS, GLA_K_DIM, GLA_V_DIM), jnp.float32)
    o_cf, s_cf = gla_chunked(gqc, gkc, gvc, gfc, s0)
    o_cb, s_cb = gla_chunked(flip(gqc), flip(gkc), flip(gvc), flip(gbc), s0)
    o_lf, _ = gla_chunked(gql, gkl, gvl, gfl, s_cf)
    o_lb, _ = gla_chunked(flip(gql), flip(gkl), flip(gvl), flip(gbl), s_cb)
    o_l = (o_lf + flip(o_lb)).astype(dt)
    g_l = rms_norm(o_l, gla_norm_g) * jax.nn.silu(gr_l.reshape(B, S, GLA_HEADS, GLA_V_DIM))

    y_lat = jnp.concatenate([a_l.reshape(B, S, DA_WIDTH), g_l.reshape(B, S, GLA_WIDTH)], -1) @ w_out
    if not with_ctx_out:
        return y_lat, None

    q_c = dq_c.reshape(B, L, DA_HEADS, 2, DA_QK_DIM)
    a_c = rms_norm(diff_attend(q_c, k_c, v_c, lam), da_subln_g) * (1.0 - lambda_init)
    o_c = (o_cf + flip(o_cb)).astype(dt)
    g_c = rms_norm(o_c, gla_norm_g) * jax.nn.silu(gr_c.reshape(B, L, GLA_HEADS, GLA_V_DIM))
    y_ctx = jnp.concatenate([a_c.reshape(B, L, DA_WIDTH), g_c.reshape(B, L, GLA_WIDTH)], -1) @ w_out
    return y_lat, y_ctx

def hier_moe(h, w_rg, b_rg, w_re, b_re, w_gate, w_up, w_down):
    T, D = h.shape
    hf = h.astype(jnp.float32)
    g_logits = hf @ w_rg.astype(jnp.float32) + b_rg.astype(jnp.float32)
    g_prob = jax.nn.softmax(g_logits, axis=-1)
    g_sel = jnp.argmax(g_logits, axis=-1)
    g_w = jnp.take_along_axis(g_prob, g_sel[:, None], axis=-1)
    e_logits = (hf @ w_re.astype(jnp.float32) + b_re.astype(jnp.float32)).reshape(
        T, N_GROUPS, EXPERTS_PER_GROUP)
    e_in_group = jnp.take_along_axis(e_logits, g_sel[:, None, None], axis=1)[:, 0]
    top_v, top_i = lax.top_k(e_in_group, TOP_K)
    weights = jax.nn.softmax(top_v, axis=-1) * g_w
    expert_id = (g_sel[:, None] * EXPERTS_PER_GROUP + top_i).astype(jnp.int32)

    tk = T * TOP_K
    n_blocks = -(-(tk + N_EXPERTS * (DISPATCH_BLOCK - 1)) // DISPATCH_BLOCK)
    n_rows = n_blocks * DISPATCH_BLOCK
    flat_e = expert_id.reshape(-1)
    flat_t = jnp.repeat(jnp.arange(T, dtype=jnp.int32), TOP_K)
    flat_w = weights.reshape(-1)
    order = jnp.argsort(flat_e)
    e_sorted = flat_e[order]
    counts = jnp.bincount(flat_e, length=N_EXPERTS)
    starts = jnp.cumsum(counts) - counts
    padded = ((counts + DISPATCH_BLOCK - 1) // DISPATCH_BLOCK) * DISPATCH_BLOCK
    pad_ends = jnp.cumsum(padded)
    pad_starts = pad_ends - padded
    dest = pad_starts[e_sorted] + (jnp.arange(tk) - starts[e_sorted])
    row_tok = jnp.full((n_rows,), T, jnp.int32).at[dest].set(flat_t[order])
    row_w = jnp.zeros((n_rows,), jnp.float32).at[dest].set(flat_w[order])
    block_start = jnp.arange(n_blocks, dtype=jnp.int32) * DISPATCH_BLOCK
    block_e = jnp.minimum(jnp.searchsorted(pad_ends, block_start, side="right"), N_EXPERTS - 1)
    h_pad = jnp.concatenate([h, jnp.zeros((1, D), h.dtype)], axis=0)
    xb = h_pad[row_tok].reshape(n_blocks, DISPATCH_BLOCK, D)

    def expert_block(args):
        xi, e = args
        return (jax.nn.silu(xi @ w_gate[e]) * (xi @ w_up[e])) @ w_down[e]

    yb = lax.map(expert_block, (xb, block_e)).reshape(n_rows, D)
    y = jax.ops.segment_sum(yb * row_w[:, None].astype(yb.dtype), row_tok, num_segments=T + 1)
    return y[:T]

def first_inputs(seed: int = 0) -> dict:
    key = jax.random.key(seed)
    ks = jax.random.split(key, 24)
    f32 = jnp.float32
    D = D_MODEL
    nrm = lambda k, shape, s: jax.random.normal(k, shape, f32) * s
    gain = lambda k, shape: 1.0 + 0.02 * jax.random.normal(k, shape, f32)
    return {
        "x": nrm(ks[0], (BATCH, SEQ, D), 1.0),
        "c": nrm(ks[1], (BATCH, D), 1.0),
        "ctx": nrm(ks[2], (BATCH, CTX_LEN, D), 1.0),
        "c_ctx": nrm(ks[3], (D,), 1.0),
        "w_ada": nrm(ks[4], (DEPTH, D, 6 * D), 0.5 * D ** -0.5),
        "b_ada": nrm(ks[5], (DEPTH, 6 * D), 0.02),
        "norm_mix_g": gain(ks[6], (DEPTH, D)),
        "norm_ffn_g": gain(ks[7], (DEPTH, D)),
        "w_in": nrm(ks[8], (DEPTH, D, IN_PROJ_DIM), D ** -0.5),
        "da_lambda": nrm(ks[9], (DEPTH, 4, DA_QK_DIM), 0.1),
        "da_subln_g": gain(ks[10], (DEPTH, DA_V_DIM)),
        "gla_gate_w2": nrm(ks[11], (DEPTH, 2, GLA_GATE_RANK, GLA_HEADS * GLA_K_DIM), GLA_GATE_RANK ** -0.5),
        "gla_gate_b": nrm(ks[12], (DEPTH, 2, GLA_HEADS * GLA_K_DIM), 0.1),
        "gla_norm_g": gain(ks[13], (DEPTH, GLA_V_DIM)),
        "w_out": nrm(ks[14], (DEPTH, MIX_WIDTH, D), MIX_WIDTH ** -0.5),
        "router_group_w": nrm(ks[15], (DEPTH, D, N_GROUPS), D ** -0.5),
        "router_group_b": nrm(ks[16], (DEPTH, N_GROUPS), 0.01),
        "router_expert_w": nrm(ks[17], (DEPTH, D, N_EXPERTS), D ** -0.5),
        "router_expert_b": nrm(ks[18], (DEPTH, N_EXPERTS), 0.01),
        "expert_w_gate": nrm(ks[19], (DEPTH, N_EXPERTS, D, EXPERT_HIDDEN), D ** -0.5),
        "expert_w_up": nrm(ks[20], (DEPTH, N_EXPERTS, D, EXPERT_HIDDEN), D ** -0.5),
        "expert_w_down": nrm(ks[21], (DEPTH, N_EXPERTS, EXPERT_HIDDEN, D), EXPERT_HIDDEN ** -0.5),
        "final_norm_g": gain(ks[22], (D,)),
    }

def first_block(x, c, ctx, c_ctx, w_ada, b_ada, norm_mix_g, norm_ffn_g, w_in, da_lambda,
              da_subln_g, gla_gate_w2, gla_gate_b, gla_norm_g, w_out, router_group_w,
              router_group_b, router_expert_w, router_expert_b, expert_w_gate, expert_w_up,
              expert_w_down, final_norm_g):
    B, S, D = x.shape
    L = ctx.shape[1]
    rows = S // GRID_W
    cos, sin = axial_rope_tables(rows, DA_QK_DIM)
    for layer in range(DEPTH):
        last = layer == DEPTH - 1
        lambda_init = 0.8 - 0.6 * math.exp(-0.3 * layer)
        mod_lat = (jax.nn.silu(c) @ w_ada[layer] + b_ada[layer])[:, None, :]
        mod_ctx = jax.nn.silu(c_ctx) @ w_ada[layer] + b_ada[layer]
        sh1, sc1, gt1, sh2, sc2, gt2 = jnp.split(mod_lat, 6, axis=-1)
        csh1, csc1, cgt1, csh2, csc2, cgt2 = jnp.split(mod_ctx, 6, axis=-1)

        h_lat = modulate(rms_norm(x, norm_mix_g[layer]), sh1, sc1)
        h_ctx = modulate(rms_norm(ctx, norm_mix_g[layer]), csh1, csc1)
        y_lat, y_ctx = token_mixer(h_lat, h_ctx, cos, sin, lambda_init, w_in[layer],
                                   da_lambda[layer], da_subln_g[layer], gla_gate_w2[layer],
                                   gla_gate_b[layer], gla_norm_g[layer], w_out[layer],
                                   with_ctx_out=not last)
        x = x + gt1 * y_lat

        moe_args = (router_group_w[layer], router_group_b[layer], router_expert_w[layer],
                    router_expert_b[layer], expert_w_gate[layer], expert_w_up[layer],
                    expert_w_down[layer])
        h2 = modulate(rms_norm(x, norm_ffn_g[layer]), sh2, sc2)
        x = x + gt2 * hier_moe(h2.reshape(B * S, D), *moe_args).reshape(B, S, D)
        if not last:
            ctx = ctx + cgt1 * y_ctx
            hc2 = modulate(rms_norm(ctx, norm_ffn_g[layer]), csh2, csc2)
            ctx = ctx + cgt2 * hier_moe(hc2.reshape(B * L, D), *moe_args).reshape(B, L, D)
    return rms_norm(x, final_norm_g)


D_RNN = 1024
RNN_BLOCKS = 8
RNN_BLOCK_W = D_RNN // RNN_BLOCKS
CONV_W = 4
LRU_C = 8.0
N_HEADS = 8
QK_NOPE = 128
QK_ROPE = 64
QK_DIM = QK_NOPE + QK_ROPE
V_DIM = 128
Q_LORA = 256
KV_LORA = 256
ROPE_THETA = 10000.0
N_GROUPS_2 = 8
N_EXPERTS_2 = N_GROUPS_2 * EXPERTS_PER_GROUP
D_EXPERT = 256
MOE_BLOCK = 128
EPS = 1e-6

IN_SPLITS = (D_RNN, D_RNN, Q_LORA, KV_LORA, QK_ROPE, D_MODEL, D_MODEL)
D_IN = D_RNN + D_RNN + Q_LORA + KV_LORA + QK_ROPE + D_MODEL + D_MODEL


def rmsnorm(x, g):
    xf = x.astype(jnp.float32)
    y = xf * lax.rsqrt(jnp.mean(xf * xf, axis=-1, keepdims=True) + EPS)
    return (y * g.astype(jnp.float32)).astype(x.dtype)

def causal_depthwise_conv(x, w, b):
    y = lax.conv_general_dilated(
        x, w[:, None, :].astype(x.dtype), window_strides=(1,),
        padding=[(CONV_W - 1, 0)], dimension_numbers=("NWC", "WIO", "NWC"),
        feature_group_count=x.shape[-1])
    return y + b.astype(x.dtype)

def rg_lru(x, wa, ba, wx, bx, lam):
    B, S, C = x.shape
    xb = x.reshape(B, S, RNN_BLOCKS, RNN_BLOCK_W)
    r = jax.nn.sigmoid(jnp.einsum("bsnk,nkj->bsnj", xb, wa).reshape(B, S, C) + ba)
    i = jax.nn.sigmoid(jnp.einsum("bsnk,nkj->bsnj", xb, wx).reshape(B, S, C) + bx)
    log_a = -LRU_C * r.astype(jnp.float32) * jax.nn.softplus(-lam.astype(jnp.float32))
    a = jnp.exp(log_a)
    mult = jnp.sqrt(-jnp.expm1(2.0 * log_a))
    b_in = x.astype(jnp.float32) * i.astype(jnp.float32) * mult

    def combine(left, right):
        a1, b1 = left
        a2, b2 = right
        return a1 * a2, a2 * b1 + b2

    _, h = lax.associative_scan(combine, (a, b_in), axis=1)
    return h.astype(x.dtype)

def apply_rope(x, cos, sin):
    half = x.shape[-1] // 2
    x1, x2 = x[..., :half], x[..., half:]
    return jnp.concatenate([x1 * cos - x2 * sin, x2 * cos + x1 * sin], axis=-1)

def mla_attention(c_q, c_kv, k_pe, positions, q_norm_g, w_uq, kv_norm_g, w_ukv,
                  qk_q_g, qk_k_g, w_mla_o):
    B, S, _ = c_q.shape
    q = (rmsnorm(c_q, q_norm_g) @ w_uq).reshape(B, S, N_HEADS, QK_DIM)
    kv = (rmsnorm(c_kv, kv_norm_g) @ w_ukv).reshape(B, S, N_HEADS, QK_NOPE + V_DIM)
    k_nope, v = kv[..., :QK_NOPE], kv[..., QK_NOPE:]
    k_pe_h = jnp.broadcast_to(k_pe[:, :, None, :], (B, S, N_HEADS, QK_ROPE))
    k = jnp.concatenate([k_nope, k_pe_h], axis=-1)
    q = rmsnorm(q, qk_q_g)
    k = rmsnorm(k, qk_k_g)
    inv_freq = ROPE_THETA ** (-jnp.arange(0, QK_ROPE, 2, dtype=jnp.float32) / QK_ROPE)
    ang = positions.astype(jnp.float32)[..., None] * inv_freq
    cos = jnp.cos(ang)[:, :, None, :].astype(q.dtype)
    sin = jnp.sin(ang)[:, :, None, :].astype(q.dtype)
    q = jnp.concatenate([q[..., :QK_NOPE], apply_rope(q[..., QK_NOPE:], cos, sin)], axis=-1)
    k = jnp.concatenate([k[..., :QK_NOPE], apply_rope(k[..., QK_NOPE:], cos, sin)], axis=-1)
    scale = QK_DIM ** -0.5
    outs = []
    for s0 in range(0, S, Q_BLOCK):
        e = s0 + Q_BLOCK
        s = jnp.einsum("bqhd,bkhd->bhqk", q[:, s0:e], k[:, :e]).astype(jnp.float32) * scale
        mask = jnp.arange(e)[None, :] <= (s0 + jnp.arange(Q_BLOCK))[:, None]
        p = jax.nn.softmax(jnp.where(mask, s, -jnp.inf), axis=-1).astype(v.dtype)
        outs.append(jnp.einsum("bhqk,bkhd->bqhd", p, v[:, :e]))
    o = jnp.concatenate(outs, axis=1).reshape(B, S, N_HEADS * V_DIM)
    return o @ w_mla_o

def hier_moe_2(u, wg, bg, we, be, w1, w3, w2):
    B, S, D = u.shape
    N = B * S
    xf = u.reshape(N, D)
    g_logits = (xf @ wg).astype(jnp.float32) + bg.astype(jnp.float32)
    g_prob = jax.nn.softmax(g_logits, axis=-1)
    g_sel = jnp.argmax(g_logits, axis=-1).astype(jnp.int32)
    e_logits = ((xf @ we).astype(jnp.float32) + be.astype(jnp.float32)).reshape(N, N_GROUPS_2, EXPERTS_PER_GROUP)
    e_in_group = jnp.take_along_axis(e_logits, g_sel[:, None, None], axis=1)[:, 0]
    e_prob = jax.nn.softmax(e_in_group, axis=-1)
    top_p, top_j = lax.top_k(e_prob, TOP_K)
    gate = jnp.take_along_axis(g_prob, g_sel[:, None], axis=1) * top_p / jnp.sum(top_p, axis=-1, keepdims=True)
    expert_id = g_sel[:, None] * EXPERTS_PER_GROUP + top_j.astype(jnp.int32)
    M = N * TOP_K
    flat_e = expert_id.reshape(M)
    flat_tok = jnp.repeat(jnp.arange(N, dtype=jnp.int32), TOP_K)
    flat_w = gate.reshape(M)
    order = jnp.argsort(flat_e)
    sorted_e = flat_e[order]
    counts = jnp.bincount(flat_e, length=N_EXPERTS_2)
    padded = ((counts + MOE_BLOCK - 1) // MOE_BLOCK) * MOE_BLOCK
    start = jnp.cumsum(counts) - counts
    pad_end = jnp.cumsum(padded)
    pad_start = pad_end - padded
    dest = pad_start[sorted_e] + (jnp.arange(M, dtype=jnp.int32) - start[sorted_e])
    m_pad = M + N_EXPERTS_2 * MOE_BLOCK
    n_blocks = m_pad // MOE_BLOCK
    tok_buf = jnp.full((m_pad,), N, dtype=jnp.int32).at[dest].set(flat_tok[order])
    w_buf = jnp.zeros((m_pad,), dtype=jnp.float32).at[dest].set(flat_w[order])
    block_e = jnp.minimum(
        jnp.searchsorted(pad_end, jnp.arange(n_blocks, dtype=jnp.int32) * MOE_BLOCK, side="right"),
        N_EXPERTS_2 - 1).astype(jnp.int32)
    x_pad = jnp.concatenate([xf, jnp.zeros((1, D), xf.dtype)], axis=0)[tok_buf]
    x_pad = x_pad.reshape(n_blocks, MOE_BLOCK, D)

    def expert_block(args):
        xb, e = args
        h = jax.nn.silu(xb @ w1[e]) * (xb @ w3[e])
        return h @ w2[e]

    y_pad = lax.map(expert_block, (x_pad, block_e)).reshape(m_pad, D)
    y = jax.ops.segment_sum(y_pad * w_buf[:, None].astype(y_pad.dtype), tok_buf, num_segments=N + 1)[:N]
    return y.reshape(B, S, D)

def second_inputs(seed: int = 0) -> dict:
    key = jax.random.key(seed)
    ks = jax.random.split(key, 32)
    L, D, f32 = DEPTH, D_MODEL, jnp.float32

    def nrm(k, shape, fan_in):
        return jax.random.normal(k, shape, f32) * (fan_in ** -0.5)

    def gain(k, shape):
        return 1.0 + 0.1 * jax.random.normal(k, shape, f32)

    def bias(k, shape):
        return 0.01 * jax.random.normal(k, shape, f32)

    x = jax.random.normal(ks[0], (BATCH, SEQ, D), f32)
    offset = jax.random.randint(ks[1], (BATCH, 1), 0, 4096, dtype=jnp.int32)
    positions = offset + jnp.arange(SEQ, dtype=jnp.int32)[None, :]
    a0 = jax.random.uniform(ks[2], (L, D_RNN), f32, 0.9, 0.999)
    s0 = a0 ** (1.0 / LRU_C)
    lru_lambda = jnp.log(s0) - jnp.log1p(-s0)
    return {
        "x": x,
        "positions": positions,
        "norm1_g": gain(ks[3], (L, D)),
        "w_in": nrm(ks[4], (L, D, D_IN), D),
        "conv_w": nrm(ks[5], (L, CONV_W, D_RNN), CONV_W),
        "conv_b": bias(ks[6], (L, D_RNN)),
        "lru_wa": nrm(ks[7], (L, RNN_BLOCKS, RNN_BLOCK_W, RNN_BLOCK_W), RNN_BLOCK_W),
        "lru_ba": bias(ks[8], (L, D_RNN)),
        "lru_wx": nrm(ks[9], (L, RNN_BLOCKS, RNN_BLOCK_W, RNN_BLOCK_W), RNN_BLOCK_W),
        "lru_bx": bias(ks[10], (L, D_RNN)),
        "lru_lambda": lru_lambda,
        "w_rnn_o": nrm(ks[11], (L, D_RNN, D), D_RNN),
        "q_norm_g": gain(ks[12], (L, Q_LORA)),
        "w_uq": nrm(ks[13], (L, Q_LORA, N_HEADS * QK_DIM), Q_LORA),
        "kv_norm_g": gain(ks[14], (L, KV_LORA)),
        "w_ukv": nrm(ks[15], (L, KV_LORA, N_HEADS * (QK_NOPE + V_DIM)), KV_LORA),
        "qk_norm_q_g": gain(ks[16], (L, QK_DIM)),
        "qk_norm_k_g": gain(ks[17], (L, QK_DIM)),
        "w_mla_o": nrm(ks[18], (L, N_HEADS * V_DIM, D), N_HEADS * V_DIM),
        "w_out": nrm(ks[19], (L, D, D), D),
        "norm2_g": gain(ks[20], (L, D)),
        "router_wg": nrm(ks[21], (L, D, N_GROUPS_2), D),
        "router_bg": bias(ks[22], (L, N_GROUPS_2)),
        "router_we": nrm(ks[23], (L, D, N_EXPERTS_2), D),
        "router_be": bias(ks[24], (L, N_EXPERTS_2)),
        "exp_w1": nrm(ks[25], (L, N_EXPERTS_2, D, D_EXPERT), D),
        "exp_w3": nrm(ks[26], (L, N_EXPERTS_2, D, D_EXPERT), D),
        "exp_w2": nrm(ks[27], (L, N_EXPERTS_2, D_EXPERT, D), D_EXPERT),
    }

def second_block(x, positions, norm1_g, w_in, conv_w, conv_b, lru_wa, lru_ba, lru_wx, lru_bx,
              lru_lambda, w_rnn_o, q_norm_g, w_uq, kv_norm_g, w_ukv, qk_norm_q_g, qk_norm_k_g,
              w_mla_o, w_out, norm2_g, router_wg, router_bg, router_we, router_be,
              exp_w1, exp_w3, exp_w2):
    split_points = [int(p) for p in np.cumsum(IN_SPLITS)[:-1]]
    h = x
    for l in range(DEPTH):
        u = rmsnorm(h, norm1_g[l])
        proj = u @ w_in[l]
        x_r, y_r, c_q, c_kv, k_pe, g_a, g_b = jnp.split(proj, split_points, axis=-1)
        x_r = causal_depthwise_conv(x_r, conv_w[l], conv_b[l])
        h_r = rg_lru(x_r, lru_wa[l], lru_ba[l], lru_wx[l], lru_bx[l], lru_lambda[l])
        branch_a = (h_r * jax.nn.gelu(y_r, approximate=True)) @ w_rnn_o[l]
        branch_b = mla_attention(c_q, c_kv, k_pe, positions, q_norm_g[l], w_uq[l], kv_norm_g[l],
                                 w_ukv[l], qk_norm_q_g[l], qk_norm_k_g[l], w_mla_o[l])
        merged = jax.nn.sigmoid(g_a) * branch_a + jax.nn.sigmoid(g_b) * branch_b
        h = h + merged @ w_out[l]
        h = h + hier_moe_2(rmsnorm(h, norm2_g[l]), router_wg[l], router_bg[l], router_we[l],
                         router_be[l], exp_w1[l], exp_w3[l], exp_w2[l])
    return h


def setup_inputs(seed=0):
    out = dict(first_inputs(seed))
    for name, value in second_inputs(seed + 1).items():
        if name != "x":
            out[name + "_2"] = value
    return out


def reference(
    x, c, ctx, c_ctx, w_ada, b_ada, norm_mix_g, norm_ffn_g, w_in, da_lambda, da_subln_g,
    gla_gate_w2, gla_gate_b, gla_norm_g, w_out, router_group_w, router_group_b, router_expert_w,
    router_expert_b, expert_w_gate, expert_w_up, expert_w_down, final_norm_g, positions_2,
    norm1_g_2, w_in_2, conv_w_2, conv_b_2, lru_wa_2, lru_ba_2, lru_wx_2, lru_bx_2, lru_lambda_2,
    w_rnn_o_2, q_norm_g_2, w_uq_2, kv_norm_g_2, w_ukv_2, qk_norm_q_g_2, qk_norm_k_g_2,
    w_mla_o_2, w_out_2, norm2_g_2, router_wg_2, router_bg_2, router_we_2, router_be_2, exp_w1_2,
    exp_w3_2, exp_w2_2,
):
    x = first_block(
        x, c, ctx, c_ctx, w_ada, b_ada, norm_mix_g, norm_ffn_g, w_in, da_lambda, da_subln_g,
        gla_gate_w2, gla_gate_b, gla_norm_g, w_out, router_group_w, router_group_b,
        router_expert_w, router_expert_b, expert_w_gate, expert_w_up, expert_w_down,
        final_norm_g,
    )
    return second_block(
        x, positions_2, norm1_g_2, w_in_2, conv_w_2, conv_b_2, lru_wa_2, lru_ba_2, lru_wx_2,
        lru_bx_2, lru_lambda_2, w_rnn_o_2, q_norm_g_2, w_uq_2, kv_norm_g_2, w_ukv_2,
        qk_norm_q_g_2, qk_norm_k_g_2, w_mla_o_2, w_out_2, norm2_g_2, router_wg_2, router_bg_2,
        router_we_2, router_be_2, exp_w1_2, exp_w3_2, exp_w2_2,
    )


_drawn_inputs = setup_inputs


def setup_inputs(seed=0):
    import zlib

    import numpy as np

    out = dict(_drawn_inputs(seed))
    spreads = {}
    factors = {'norm_mix_g': 3.309,
     'norm_ffn_g': 3.288,
     'da_lambda': 6.051,
     'da_subln_g': 3.209,
     'gla_gate_b': 2.945,
     'gla_norm_g': 5.729,
     'router_group_b': 8.0,
     'router_expert_b': 4.739,
     'lru_ba_2': 46.541,
     'lru_bx_2': 33.235,
     'q_norm_g_2': 4.217,
     'qk_norm_q_g_2': 3.609,
     'qk_norm_k_g_2': 4.458,
     'router_bg_2': 13.088,
     'router_be_2': 4.722}
    for name, (base, spread) in spreads.items():
        noise = np.random.default_rng([zlib.crc32(name.encode()), seed]).standard_normal(out[name].shape)
        drawn = base * np.exp(spread * noise) if base else spread * noise
        out[name] = jnp.asarray(drawn.astype(out[name].dtype))
    for name, factor in factors.items():
        out[name] = (out[name] * factor).astype(out[name].dtype)
    return out
```

```python
from contextlib import ExitStack

import numpy as np
import concourse.bass as bass
from concourse import mybir

P = 128
F32 = mybir.dt.float32
F32R = mybir.dt.float32r
I32 = mybir.dt.int32
U32 = mybir.dt.uint32
ALU = mybir.AluOpType
ACT = mybir.ActivationFunctionType
AX_X = mybir.AxisListType.X

BANK = 512
D = 1024
KD = D // P
T = 1024
TT = T // P
EPS = 1e-6


class Chain:

    def __init__(self, eng, sem):
        self.eng, self.sem, self.n, self.base = eng, sem, 0, 0

    def mark(self, ins):
        ins.then_inc(self.sem, 1)
        self.n += 1

    def settle(self):
        self.eng.wait_ge(self.sem, self.base + self.n)

    def link(self, ins):
        self.mark(ins)
        self.settle()

    def turn(self, base):
        self.base, self.n = base, 0


class Core:

    def __init__(self, nc, ctx):
        self.nc, self.ctx, self.stage_sems = nc, ctx, []

    def sem(self, name):
        s = self.nc.alloc_semaphore(name)
        self.stage_sems.append(s)
        return s

    def end_stage(self):
        self.nc.clear_and_free_semaphores(self.stage_sems)
        self.stage_sems = []
        self.nc.all_engine_barrier()

    def keep(self, name, shape, dt=F32):
        return self.ctx.enter_context(self.nc.sbuf_tensor(name, shape, dt))


def constants(core):
    nc = core.nc
    core.ident = core.keep("ident", [P, P])
    core.eps = core.keep("eps", [P, 1])
    core.ones = core.keep("ones", [P, P])
    core.chunk_incl = core.keep("chunk_incl", [P, P])
    core.chunk_suffix = core.keep("chunk_suffix", [P, P])
    core.before = core.keep("before", [P, P])
    core.causal = core.keep("causal", [P, P])


def column_vectors(core, name, rows, evac=None):
    nc = core.nc
    total = sum(r.shape[0] for _, r in rows)
    assert total <= P
    table = core.keep(f"{name}_cols", [P, total])
    at = {}
    loaded = core.sem(f"{name}_loaded")
    turned = core.sem(f"{name}_turned")
    copied = core.sem(f"{name}_copied")
    with ExitStack() as ctx:
        flat = ctx.enter_context(nc.sbuf_tensor(f"{name}_rows", [P, P], F32))
        ps = ctx.enter_context(nc.psum_tensor(f"{name}_ps", [P, BANK], F32))
        with nc.Block() as block:

            @block.sync
            def _(sp):
                n = 0
                for label, r in rows:
                    sp.dma_start(flat[n:n + r.shape[0], :], r).then_inc(loaded, 16)
                    at[label] = slice(n, n + r.shape[0])
                    n += r.shape[0]

            @block.tensor
            def _(pe):
                pe.wait_ge(loaded, 16 * len(rows))
                nc.tensor.transpose(ps[:, 0:total], flat[0:total, :], core.ident[0:total, 0:total]).then_inc(turned, 1)

            @block.vector
            def _(dve):
                dve.wait_ge(turned, 1)
                nc.vector.tensor_copy(table[:, :], ps[:, 0:total]).then_inc(copied, 1)
                dve.wait_ge(copied, 1)
    return table, at


def build_constants(core, inp):
    nc = core.nc
    constants(core)
    made = core.sem("constants_made")
    n_made = [0]
    with nc.Block() as block:

        @block.gpsimd
        def _(pool):
            def step(ins):
                ins.then_inc(made, 1)
                n_made[0] += 1
                pool.wait_ge(made, n_made[0])

            step(nc.gpsimd.memset(core.ones[:], 1.0))
            step(nc.gpsimd.memset(core.eps[:], EPS))
            step(nc.gpsimd.memset(core.ident[:], 0.0))
            step(nc.gpsimd.affine_select(out=core.ident[:], in_=core.ident[:], compare_op=ALU.not_equal, fill=1.0,
                                         base=0, pattern=[[-1, P]], channel_multiplier=1))
            step(nc.gpsimd.affine_select(out=core.before[:], in_=core.ones[:], compare_op=ALU.is_gt, fill=0.0,
                                         base=0, pattern=[[1, P]], channel_multiplier=-1))
            step(nc.gpsimd.affine_select(out=core.causal[:], in_=core.ones[:], compare_op=ALU.is_ge, fill=0.0,
                                         base=0, pattern=[[-1, P]], channel_multiplier=1))
            step(nc.gpsimd.affine_select(out=core.chunk_incl[:], in_=core.ones[:], compare_op=ALU.is_ge, fill=0.0,
                                         base=0, pattern=[[1, P]], channel_multiplier=-1))
            step(nc.gpsimd.affine_select(out=core.chunk_suffix[:], in_=core.ones[:], compare_op=ALU.is_ge, fill=0.0,
                                         base=0, pattern=[[-1, P]], channel_multiplier=1))
            step(nc.gpsimd.memset(core.chunk_incl[0:64, 64:128], 0.0))
            step(nc.gpsimd.memset(core.chunk_suffix[64:128, 0:64], 0.0))


def modulation(core, inp):
    nc = core.nc
    NC = 6 * KD
    SLAB = 512
    core.mods = core.keep("mods", [P, 2, NC])
    core.mix_scale = core.keep("mix_scale", [P, 2, KD])
    core.ffn_scale = core.keep("ffn_scale", [P, KD])
    core.gate_rows = core.keep("gate_rows", [P, 2, D])
    n_slabs = 6 * D // SLAB
    per = SLAB // P
    w = inp["w_ada"][0].rearrange("(k p) n -> p k n", p=P)
    w_loaded = [core.sem(f"ada_w_loaded{b}") for b in range(2)]
    w_used = core.sem("ada_w_used")
    c_ready = core.sem("ada_c_ready")
    own = core.sem("ada_dve")
    diag_ready = core.sem("ada_diag_ready")
    row_done = core.sem("ada_row_done")
    row_copied = core.sem("ada_row_copied")
    with ExitStack() as ctx:
        slab = ctx.enter_context(nc.sbuf_tensor("ada_slab", [P, 2, KD, SLAB], F32))
        cs = ctx.enter_context(nc.sbuf_tensor("ada_cs", [P, 2, KD], F32))
        diag = ctx.enter_context(nc.sbuf_tensor("ada_diag", [P, 2, KD, P], F32))
        ps = ctx.enter_context(nc.psum_tensor("ada_ps", [P, BANK], F32))
        psr = ctx.enter_context(nc.psum_tensor("ada_psr", [P, 4, BANK], F32))
        v, at = core.v1, core.at1
        with nc.Block() as block:

            @block.sync
            def _(sp):
                for s in range(n_slabs):
                    if s >= 2:
                        sp.wait_ge(w_used, s - 1)
                    sp.dma_start(slab[:, s % 2], w[:, :, s * SLAB:(s + 1) * SLAB]).then_inc(w_loaded[s % 2], 16)

            @block.scalar
            def _(act):
                nc.scalar.activation(cs[:, 0], v[:, at["c"]], ACT.Silu).then_inc(c_ready, 1)
                nc.scalar.activation(cs[:, 1], v[:, at["c_ctx"]], ACT.Silu).then_inc(c_ready, 1)

            @block.tensor
            def _(pe):
                pe.wait_ge(c_ready, 2)
                for s in range(n_slabs):
                    pe.wait_ge(w_loaded[s % 2], 16 * (s // 2 + 1))
                    for f in range(per):
                        col = 2 * (s * per + f)
                        for k in range(KD):
                            last = nc.tensor.matmul(ps[:, col:col + 2], slab[:, s % 2, k, f * P:(f + 1) * P],
                                                    cs[:, :, k], start=(k == 0), stop=(k == KD - 1))
                    last.then_inc(w_used, 1)
                pe.wait_ge(diag_ready, 2 * KD)
                for g in range(2):
                    for k in range(KD):
                        last = nc.tensor.matmul(psr[:, 2 * g + k // 4, (k % 4) * P:(k % 4 + 1) * P], core.ones[:],
                                                diag[:, g, k], start=True, stop=True)
                last.then_inc(row_done, 1)

            @block.vector
            def _(dve):
                ch = Chain(dve, own)
                dve.wait_ge(w_used, n_slabs)
                for j in range(2):
                    ch.mark(nc.vector.tensor_tensor(core.mods[:, j], ps[:, j:2 * NC:2], v[:, at["b_ada"]], ALU.add))
                ch.settle()
                for j in range(2):
                    ch.mark(nc.vector.scalar_tensor_tensor(core.mix_scale[:, j], core.mods[:, j, KD:2 * KD], 1.0,
                                                           v[:, at["norm_mix_g"]], ALU.add, ALU.mult))
                ch.mark(nc.vector.scalar_tensor_tensor(core.ffn_scale[:], core.mods[:, 0, 4 * KD:5 * KD], 1.0,
                                                       v[:, at["norm_ffn_g"]], ALU.add, ALU.mult))
                for g in range(2):
                    for k in range(KD):
                        c = (2 + 3 * g) * KD + k
                        nc.vector.tensor_scalar(diag[:, g, k], core.ident[:], core.mods[:, 0, c:c + 1], None,
                                                ALU.mult).then_inc(diag_ready, 1)
                dve.wait_ge(row_done, 1)
                nc.vector.tensor_copy(core.gate_rows[:, :, :], psr[:, :, :].rearrange("p (g a) n -> p g (a n)", g=2)) \
                    .then_inc(row_copied, 1)
                dve.wait_ge(row_copied, 1)
                ch.settle()


def pair(core, ctx, name, shape):
    return [ctx.enter_context(core.nc.sbuf_tensor(f"{name}_{part}", shape, F32R)) for part in ("high", "low")]


def low_part(nc, low, x, high):
    return nc.vector.tensor_tensor(low, x, high.bitcast(F32), ALU.subtract)


def split_matmuls(nc, dst, terms):
    for k, (a_high, a_low, b_high, b_low) in enumerate(terms):
        nc.tensor.matmul(dst, a_high, b_low, start=(k == 0), stop=False)
        nc.tensor.matmul(dst, a_low, b_high, start=False, stop=False)
        last = nc.tensor.matmul(dst, a_high, b_high, start=False, stop=(k == len(terms) - 1))
    return last


def norm_transpose(core, name, tiles, hT, rows_out=None, width=D):
    nc = core.nc
    n = len(tiles)
    kd = width // P
    at = lambda k: (2 * k // kd) * BANK + (k % (kd // 2)) * P
    x_loaded = [core.sem(f"{name}_x_loaded{b}") for b in range(2)]
    sum_ready = core.sem(f"{name}_sum_ready")
    own = core.sem(f"{name}_dve")
    root_ready = core.sem(f"{name}_root_ready")
    xn_ready = core.sem(f"{name}_xn_ready")
    turned = core.sem(f"{name}_turned")
    split = isinstance(hT, list)
    high_done = core.sem(f"{name}_high_done")
    low_done = core.sem(f"{name}_low_done")
    half_a = core.sem(f"{name}_half_a")
    half_v = core.sem(f"{name}_half_v")
    stored = [core.sem(f"{name}_stored{b}") for b in range(2)]
    with ExitStack() as ctx:
        xt = ctx.enter_context(nc.sbuf_tensor(f"{name}_xt", [P, 2, width], F32))
        xn = ctx.enter_context(nc.sbuf_tensor(f"{name}_xn", [P, 2, width], F32))
        st = ctx.enter_context(nc.sbuf_tensor(f"{name}_st", [P, n, 4], F32))
        if split:
            ht = ctx.enter_context(nc.sbuf_tensor(f"{name}_ht", [P, 2, kd, P], F32))
        ps = ctx.enter_context(nc.psum_tensor(f"{name}_ps", [P, 2, 2 * BANK], F32))
        with nc.Block() as block:

            @block.sync
            def _(sp):
                for i, (rows, _, _) in enumerate(tiles):
                    if i >= 2:
                        sp.wait_ge(xn_ready, i - 1)
                    sp.dma_start(xt[:, i % 2], rows).then_inc(x_loaded[i % 2], 16)

            @block.gpsimd
            def _(pool):
                if rows_out is not None:
                    for i in range(n):
                        pool.wait_ge(xn_ready, i + 1)
                        pool.dma_start(rows_out[i * P:(i + 1) * P, :], xn[:, i % 2]).then_inc(stored[i % 2], 16)
                    for b in range(2):
                        pool.wait_ge(stored[b], 16 * (n // 2))

            def evacuate(engine_op, i, k):
                _, scale, shift = tiles[i]
                src = ps[:, i % 2, at(k):at(k) + P]
                dst = ht[:, i % 2, k, :] if split else hT[:, k, i * P:(i + 1) * P]
                return engine_op(dst, src, scale[:, k:k + 1], None if shift is None else shift[:, k:k + 1])

            @block.vector
            def _(dve):
                ch = Chain(dve, own)

                def op(dst, src, scale, shift):
                    return nc.vector.tensor_scalar(dst, src, scale, shift, ALU.mult,
                                                   *([ALU.add] if shift is not None else []))

                def normalise(i):
                    dve.wait_ge(x_loaded[i % 2], 16 * (i // 2 + 1))
                    if i >= 2:
                        dve.wait_ge(turned, i - 1)
                        if rows_out is not None:
                            dve.wait_ge(stored[i % 2], 16 * (i // 2))
                    x = xt[:, i % 2]
                    nc.vector.tensor_tensor_reduce(xn[:, i % 2], x, x, 1.0, 0.0, ALU.mult, ALU.add,
                                                   st[:, i, 0:1]).then_inc(sum_ready, 1)
                    dve.wait_ge(root_ready, i + 1)
                    ch.link(nc.vector.reciprocal(st[:, i, 2:3], st[:, i, 1:2]))
                    nc.vector.tensor_scalar(xn[:, i % 2], x, st[:, i, 2:3], None, ALU.mult) \
                        .then_inc(xn_ready, 1)

                for i in range(n + 1):
                    if i < n:
                        normalise(i)
                    if split and i >= 2:
                        dve.wait_ge(high_done, i - 1)
                        low_part(nc, hT[1][:, :, (i - 2) * P:(i - 1) * P], ht[:, i % 2],
                                 hT[0][:, :, (i - 2) * P:(i - 1) * P]).then_inc(low_done, 1)
                    if i >= 1:
                        dve.wait_ge(turned, i)
                        if split and i >= 3:
                            dve.wait_ge(low_done, i - 2)
                        for k in range(kd // 2, kd):
                            last = evacuate(op, i - 1, k)
                        last.then_inc(half_v, 1)
                if split:
                    dve.wait_ge(high_done, n)
                    low_part(nc, hT[1][:, :, (n - 1) * P:n * P], ht[:, (n - 1) % 2],
                             hT[0][:, :, (n - 1) * P:n * P]).then_inc(low_done, 1)
                    dve.wait_ge(low_done, n)
                dve.wait_ge(half_v, n)

            @block.scalar
            def _(act):
                def op(dst, src, scale, shift):
                    return nc.scalar.activation(dst, src, ACT.Identity, scale=scale,
                                                bias=0.0 if shift is None else shift)

                for i in range(n + 1):
                    if i < n:
                        act.wait_ge(sum_ready, i + 1)
                        nc.scalar.activation(st[:, i, 1:2], st[:, i, 0:1], ACT.Sqrt, scale=1.0 / width,
                                             bias=core.eps[:]).then_inc(root_ready, 1)
                    if i >= 1:
                        act.wait_ge(turned, i)
                        if split and i >= 3:
                            act.wait_ge(low_done, i - 2)
                        for k in range(kd // 2):
                            last = evacuate(op, i - 1, k)
                        last.then_inc(half_a, 1)
                        if split:
                            act.wait_ge(half_a, i)
                            act.wait_ge(half_v, i)
                            nc.scalar.copy(hT[0][:, :, (i - 1) * P:i * P], ht[:, (i - 1) % 2]).then_inc(high_done, 1)
                act.wait_ge(half_a, n)
                if split:
                    act.wait_ge(high_done, n)

            @block.tensor
            def _(pe):
                for i in range(n):
                    pe.wait_ge(xn_ready, i + 1)
                    if i >= 2:
                        pe.wait_ge(half_a, i - 1)
                        pe.wait_ge(half_v, i - 1)
                    for k in range(kd):
                        last = nc.tensor.transpose(ps[:, i % 2, at(k):at(k) + P], xn[:, i % 2, k * P:(k + 1) * P],
                                                   core.ident[:])
                    last.then_inc(turned, 1)


def linear(core, name, h, kc, tokens, w, out, features_first, n_slabs, tail=0, S=512):
    nc = core.nc
    assert n_slabs % 2 == 0
    per = (S // P) * (tokens // BANK) if features_first else tokens // P
    BUF = 4
    assert per % 2 == 0 and (2 * per) % BUF == 0
    wv = w.rearrange("(k p) n -> p k n", p=P)
    split_h = not isinstance(h, list)
    chunk = max(1, kc // 4)
    PARTS = kc // chunk
    assert PARTS % 2 == 0
    h_high = core.sem(f"{name}_h_high")
    h_split = core.sem(f"{name}_h_split")
    w_loaded = [core.sem(f"{name}_w_loaded{b}") for b in range(2)]
    w_high = core.sem(f"{name}_w_high")
    w_split = core.sem(f"{name}_w_split")
    summed = core.sem(f"{name}_summed")
    copied = [core.sem(f"{name}_copied_act"), core.sem(f"{name}_copied_dve")]
    stored = [core.sem(f"{name}_stored{b}") for b in range(BUF)]
    turns = n_slabs // 2
    total = n_slabs * per + (per if tail else 0)
    with ExitStack() as ctx:
        raw = ctx.enter_context(nc.sbuf_tensor(f"{name}_slab", [P, 2, chunk, S], F32))
        high, low = pair(core, ctx, f"{name}_w", [P, 2, kc, S])
        hh, hl = pair(core, ctx, f"{name}_h", [P, kc, tokens]) if split_h else h
        stage = ctx.enter_context(nc.sbuf_tensor(f"{name}_stage", [P, BUF, BANK], F32))
        ps = ctx.enter_context(nc.psum_tensor(f"{name}_ps", [P, BUF, BANK], F32))
        with nc.Block() as block:

            @block.sync
            def _(sp):
                def load(s, width):
                    for i in range(PARTS):
                        sp.wait_ge(w_split, s * PARTS + (i + 1))
                        sp.dma_start(raw[:, i % 2, :, 0:width],
                                     wv[:, i * chunk:(i + 1) * chunk, bass.ds(s * S, width)]) \
                            .then_inc(w_loaded[i % 2], 16)

                with sp.Fori(0, turns) as it:
                    for b in range(2):
                        load(it * 2 + b, S)
                if tail:
                    load(n_slabs, tail)

            @block.tensor
            def _(pe):
                pe.sem_inc(summed, 2 * per)
                if split_h:
                    pe.wait_ge(h_split, kc)

                def slab_items(turn, b, width):
                    pe.wait_ge(w_split, turn * (2 * PARTS) + ((b + 1) * PARTS + 2))
                    for j in range(per):
                        n = b * per + j
                        pe.wait_ge(copied[n % 2], turn * per + (n // 2 + 1))
                        if features_first:
                            f, th = j // (tokens // BANK), j % (tokens // BANK)
                            cols, toks = slice(f * P, (f + 1) * P), slice(th * BANK, (th + 1) * BANK)
                            last = split_matmuls(nc, ps[:, n % BUF, :],
                                                 [(high[:, b, k, cols], low[:, b, k, cols],
                                                   hh[:, k, toks], hl[:, k, toks]) for k in range(kc)])
                        else:
                            toks = slice(j * P, (j + 1) * P)
                            last = split_matmuls(nc, ps[:, n % BUF, 0:width],
                                                 [(hh[:, k, toks], hl[:, k, toks],
                                                   high[:, b, k, 0:width], low[:, b, k, 0:width])
                                                  for k in range(kc)])
                        last.then_inc(summed, 1)

                with pe.Fori(0, turns) as it:
                    for b in range(2):
                        slab_items(it, b, S)
                if tail:
                    slab_items(turns, 0, tail)

            def copy_item(eng, copy, turn, n, width):
                eng.wait_ge(summed, turn * (2 * per) + (2 * per + n + 1))
                eng.wait_ge(stored[n % BUF], (turn * (2 * per // BUF) + (n // BUF + 1)) * 16)
                width = BANK if features_first else width
                copy(stage[:, n % BUF, 0:width], ps[:, n % BUF, 0:width]).then_inc(copied[n % 2], 1)

            @block.scalar
            def _(act):
                act.sem_inc(copied[0], 2)
                for b in range(BUF):
                    act.sem_inc(stored[b], 16)

                def high_slab(turn, b, width):
                    act.wait_ge(summed, turn * (2 * per) + (b + 1) * per)
                    for i in range(PARTS):
                        act.wait_ge(w_loaded[i % 2], (turn * PARTS + (b * (PARTS // 2) + i // 2 + 1)) * 16)
                        nc.scalar.copy(high[:, b, i * chunk:(i + 1) * chunk, 0:width], raw[:, i % 2, :, 0:width]) \
                            .then_inc(w_high, 1)

                def items(turn, b, s, width, then=None):
                    for j in range(per):
                        n = b * per + j
                        if j == per // 2 and then is not None:
                            high_slab(*then)
                        if n % 2 == 0:
                            copy_item(act, nc.scalar.copy, turn, n, width)
                        act.wait_ge(copied[n % 2], turn * per + (n // 2 + 3))
                        if features_first:
                            f, th = j // (tokens // BANK), j % (tokens // BANK)
                            dst = out[bass.ds(s * S + f * P, P), th * BANK:(th + 1) * BANK]
                        else:
                            dst = out[j * P:(j + 1) * P, bass.ds(s * S, width)]
                        act.dma_start(dst, stage[:, n % BUF, 0:BANK if features_first else width]) \
                            .then_inc(stored[n % BUF], 16)

                if split_h:
                    for k in range(kc):
                        nc.scalar.copy(hh[:, k], h[:, k]).then_inc(h_high, 1)
                high_slab(0, 0, S)
                if turns > 1:
                    with act.Fori(0, turns - 1) as it:
                        items(it, 0, it * 2, S, (it, 1, S))
                        items(it, 1, it * 2 + 1, S, (it + 1, 0, S))
                items(turns - 1, 0, n_slabs - 2, S, (turns - 1, 1, S))
                items(turns - 1, 1, n_slabs - 1, S, (turns, 0, tail) if tail else None)
                if tail:
                    items(turns, 0, n_slabs, tail)
                for b in range(BUF):
                    act.wait_ge(stored[b], 16 * (len(range(b, total, BUF)) + 1))

            @block.vector
            def _(dve):
                dve.sem_inc(copied[1], 2)
                dve.sem_inc(w_split, 2)

                def low_slab(turn, b, width):
                    for i in range(PARTS):
                        part = slice(i * chunk, (i + 1) * chunk)
                        dve.wait_ge(w_high, turn * (2 * PARTS) + (b * PARTS + i + 1))
                        low_part(nc, low[:, b, part, 0:width], raw[:, i % 2, :, 0:width],
                                 high[:, b, part, 0:width]).then_inc(w_split, 1)

                def items(turn, b, width, then=None):
                    for j in range(per):
                        n = b * per + j
                        if j == per // 2 and then is not None:
                            low_slab(*then)
                        if n % 2 == 1:
                            copy_item(dve, nc.vector.tensor_copy, turn, n, width)

                if split_h:
                    for k in range(kc):
                        dve.wait_ge(h_high, k + 1)
                        low_part(nc, hl[:, k], h[:, k], hh[:, k]).then_inc(h_split, 1)
                low_slab(0, 0, S)
                if turns > 1:
                    with dve.Fori(0, turns - 1) as it:
                        items(it, 0, S, (it, 1, S))
                        items(it, 1, S, (it + 1, 0, S))
                items(turns - 1, 0, S, (turns - 1, 1, S))
                items(turns - 1, 1, S, (turns, 0, tail) if tail else None)
                if tail:
                    items(turns, 0, tail)


def vector_tables(core, inp):
    rows = lambda a: a.rearrange("(n p) -> n p", p=P)
    core.v1, core.at1 = column_vectors(core, "v1", [
        ("b_ada", rows(inp["b_ada"][0])), ("norm_mix_g", rows(inp["norm_mix_g"][0])),
        ("norm_ffn_g", rows(inp["norm_ffn_g"][0])), ("c", rows(inp["c"][0])), ("c_ctx", rows(inp["c_ctx"]))])


def in_projection(core, inp, proj):
    nc = core.nc
    with ExitStack() as ctx:
        n_ctx = inp["ctx"].shape[1] // P
        hT = pair(core, ctx, "h1T", [P, KD, (n_ctx + TT) * P])
        shift = [core.mods[:, j, 0:KD] for j in range(2)]
        tiles = [(inp["ctx"][0, i * P:(i + 1) * P, :], core.mix_scale[:, 1], shift[1]) for i in range(n_ctx)]
        tiles += [(inp["x"][0, i * P:(i + 1) * P, :], core.mix_scale[:, 0], shift[0]) for i in range(TT)]
        norm_transpose(core, "norm1", tiles, hT)
        linear(core, "inproj", hT, KD, (n_ctx + TT) * P, inp["w_in"][0], proj, False, 6, 32)


DA_H, DA_DIM, DA_V = 4, 64, 128
LAMBDA_INIT = 0.2


def diff_attention(core, inp, proj, mix):
    nc = core.nc
    NK = proj.shape[0]
    KT = NK // P
    CT = KT - TT
    SCALE = DA_DIM ** -0.5
    with ExitStack() as ctx:
        sb = lambda n, s, d=F32: ctx.enter_context(nc.sbuf_tensor("da_" + n, s, d))
        qT, kT = sb("qT", [P, DA_H, T]), sb("kT", [P, DA_H, NK])
        v = sb("v", [P, KT, DA_H * DA_V])
        o = sb("o", [P, TT, DA_H, DA_V])
        lam4 = sb("lam4", [1, 4, DA_DIM])
        lam = sb("lam", [1, 8])
        neglam = sb("neglam", [P, 1])
        g = sb("g", [P, DA_V])
        diff_prepare(core, inp, proj, qT, kT, v, lam4, lam, neglam, g, CT, KT)

        s_done = core.sem("da_scores_done")
        e_done = core.sem("da_exp_done")
        nb_ready = core.sem("da_bias_ready")
        a_ready = core.sem("da_a_ready")
        a_turned = core.sem("da_a_turned")
        a_copied = [core.sem("da_a_copied_act"), core.sem("da_a_copied_dve")]
        o_done = core.sem("da_o_done")
        o_read = core.sem("da_o_read")
        q_ready = core.sem("da_q_ready")
        own = core.sem("da_dve")
        U = 2 * DA_H
        GROUPS = [range(c, min(c + 4, KT)) for c in range(0, KT, 4)]
        G = len(GROUPS)
        COPIER = [0 if gi < G - 1 else 1 for gi in range(G)]
        PER = [COPIER.count(0), COPIER.count(1)]
        with ExitStack() as c2:
            s2 = lambda n, s, d=F32: c2.enter_context(nc.sbuf_tensor("da_" + n, s, d))
            p = s2("p", [P, 2, 2, NK])
            aT = s2("aT", [P, 2, KT, P])
            qcur = s2("qcur", [P, 2, DA_H, P])
            st = s2("st", [P, 2, 8])
            l0 = s2("l0", [P, 2, DA_H])
            ps = [c2.enter_context(nc.psum_tensor(f"da_s{m}", [P, 3 * BANK], F32)) for m in range(2)]
            ps_t = c2.enter_context(nc.psum_tensor("da_t", [P, BANK], F32))
            ps_o = c2.enter_context(nc.psum_tensor("da_ops", [P, DA_H, DA_V], F32))
            with nc.Block() as block:

                @block.gpsimd
                def _(pool):
                    with pool.Fori(0, TT // 2) as it:
                        for b in range(2):
                            pool.wait_ge(s_done, it * (2 * U) + 2 * DA_H * (b + 1))
                            nc.gpsimd.tensor_copy(qcur[:, b], qT[:, :, bass.ds((it * 2 + b) * P, P)]) \
                                .then_inc(q_ready, 1)

                @block.tensor
                def _(pe):
                    pe.sem_inc(s_done, 4 * DA_H)

                    def scores(it, u):
                        b, h = u // DA_H, u % DA_H
                        if h == 0:
                            pe.wait_ge(q_ready, it * 2 + (b + 1))
                        for m in range(2):
                            pe.wait_ge(e_done, it * (2 * U) + (2 * u + m + 1))
                            for n0 in range(0, NK, BANK):
                                w = min(BANK, NK - n0)
                                last = nc.tensor.matmul(ps[m][:, n0:n0 + w], qcur[64 * m:64 * m + 64, b, h, :],
                                                        kT[64 * m:64 * m + 64, h, n0:n0 + w], start=True, stop=True)
                            last.then_inc(s_done, 1)

                    def weigh(it, u):
                        b, h = u // DA_H, u % DA_H
                        pe.wait_ge(a_ready, it * U + (u + 1))

                        def copied_before(gi):
                            x = COPIER[gi - 1] if gi > 0 else 1
                            n = PER[1] if gi == 0 else PER[x] + COPIER[:gi].count(x)
                            pe.wait_ge(a_copied[x], it * (U * PER[x]) + (u * PER[x] + n))

                        def turn_group(gi):
                            copied_before(gi)
                            for j, c in enumerate(GROUPS[gi]):
                                last = nc.tensor.transpose(ps_t[:, j * P:(j + 1) * P],
                                                           p[:, u % 2, 0, c * P:(c + 1) * P], core.ident[:])
                            last.then_inc(a_turned, 1)

                        def weigh_group(gi):
                            copied_before(gi + 1)
                            for c in GROUPS[gi]:
                                last = nc.tensor.matmul(ps_o[:, h, :], aT[:, u % 2, c, :],
                                                        v[:, c, h * DA_V:(h + 1) * DA_V],
                                                        start=(c == 0), stop=(c == KT - 1))
                            return last

                        if h == 0:
                            pe.wait_ge(o_read, it * 2 + (b + 1))
                        turn_group(0)
                        for gi in range(1, G):
                            turn_group(gi)
                            weigh_group(gi - 1)
                        last = weigh_group(G - 1)
                        last.then_inc(o_done, 1)

                    with pe.Fori(0, TT // 2) as it:
                        for u in range(U + 1):
                            if u < U:
                                scores(it, u)
                            if u >= 1:
                                weigh(it, u - 1)

                def copy_turned(eng, copy, which, it, u):
                    for gi, group in enumerate(GROUPS):
                        if COPIER[gi] != which:
                            continue
                        eng.wait_ge(a_turned, it * (U * G) + (u * G + gi + 1))
                        if u >= 2:
                            eng.wait_ge(o_done, it * U + (u - 1))
                        copy(aT[:, u % 2, group[0]:group[-1] + 1, :],
                             ps_t[:, 0:len(group) * P].rearrange("p (c q) -> p c q", q=P)).then_inc(a_copied[which], 1)

                @block.scalar
                def _(act):
                    act.sem_inc(e_done, 2)
                    act.sem_inc(a_copied[0], PER[0])
                    with act.Fori(0, TT // 2) as it:
                        for u in range(U + 1):
                            if u < U:
                                b, h = u // DA_H, u % DA_H
                                for m in range(2):
                                    act.wait_ge(nb_ready, it * (2 * U) + (2 * u + m + 1))
                                    if m == 0 and u >= 2:
                                        act.wait_ge(a_turned, it * (U * G) + (u - 1) * G)
                                    sums = l0[:, b, h:h + 1] if m == 0 else st[:, u % 2, 5:6]
                                    nc.scalar.activation(p[:, u % 2, m], ps[m][:, 0:NK], ACT.Exp,
                                                         bias=st[:, u % 2, 2 + m:3 + m], scale=SCALE,
                                                         accum_out=sums).then_inc(e_done, 1)
                            if u >= 1:
                                copy_turned(act, nc.scalar.copy, 0, it, u - 1)

                @block.vector
                def _(dve):
                    ch = Chain(dve, own)
                    dve.sem_inc(a_copied[1], PER[1])
                    dve.sem_inc(o_read, 1)
                    STEPS = U * (2 + 2) + 2
                    with dve.Fori(0, TT // 2) as it:
                        ch.turn(it * STEPS)
                        for u in range(U + 1):
                            if u < U:
                                for m in range(2):
                                    dve.wait_ge(s_done, it * (2 * U) + (2 * u + m + 1 + 4 * DA_H))
                                    ch.link(nc.vector.reduce_max(st[:, u % 2, m:m + 1], ps[m][:, 0:NK], AX_X))
                                    nc.vector.tensor_scalar(st[:, u % 2, 2 + m:3 + m], st[:, u % 2, m:m + 1], -SCALE, None,
                                                            ALU.mult).then_inc(nb_ready, 1)
                            if u >= 1:
                                copy_turned(dve, nc.vector.tensor_copy, 1, it, u - 1)
                                w = u - 1
                                b, h = w // DA_H, w % DA_H
                                if h == DA_H - 1:
                                    ch.link(nc.vector.reciprocal(l0[:, b], l0[:, b]))
                                    dve.wait_ge(o_done, it * U + u)
                                    nc.vector.tensor_tensor(o[:, bass.ds(it * 2 + b, 1)].rearrange("p a h d -> p (a h) d"),
                                                            ps_o[:, :, :],
                                                            l0[:, b].unsqueeze(2).broadcast_to([P, DA_H, DA_V]),
                                                            ALU.mult).then_inc(o_read, 1)
                            if u < U:
                                b, h = u // DA_H, u % DA_H
                                dve.wait_ge(e_done, it * (2 * U) + (2 * u + 4))
                                ch.link(nc.vector.reciprocal(st[:, u % 2, 6:7], st[:, u % 2, 5:6]))
                                ch.link(nc.vector.scalar_tensor_tensor(st[:, u % 2, 7:8], st[:, u % 2, 6:7],
                                                                       l0[:, b, h:h + 1], neglam[:], ALU.mult, ALU.mult))
                                nc.vector.scalar_tensor_tensor(p[:, u % 2, 0], p[:, u % 2, 1], st[:, u % 2, 7:8],
                                                               p[:, u % 2, 0], ALU.mult, ALU.add).then_inc(a_ready, 1)
                        assert ch.n == STEPS, ch.n
        head_norm(core, "da_norm", o, g, mix[:, 0:DA_H * DA_V], None)


def head_norm(core, name, o, g, dst, gate):
    nc = core.nc
    R = TT * 4
    H4 = R // 4
    own = core.sem(f"{name}_dve")
    squared = core.sem(f"{name}_summed")
    rooted = core.sem(f"{name}_rooted")
    ready = core.sem(f"{name}_ready")
    stored = core.sem(f"{name}_stored")
    flat = o[:, :, :, :].rearrange("p t h d -> p (t h) d")
    with ExitStack() as ctx:
        sq = ctx.enter_context(nc.sbuf_tensor(f"{name}_sq", [P, R, P], F32))
        st = ctx.enter_context(nc.sbuf_tensor(f"{name}_st", [P, 3, R], F32))
        with nc.Block() as block:

            @block.vector
            def _(dve):
                ch = Chain(dve, own)
                ch.link(nc.vector.tensor_tensor(sq[:], flat, flat, ALU.mult))
                nc.vector.reduce_sum(st[:, 0], sq[:], AX_X).then_inc(squared, 1)
                dve.wait_ge(rooted, 1)
                ch.link(nc.vector.reciprocal(st[:, 2], st[:, 1]))
                ch.link(nc.vector.tensor_tensor(sq[:], flat, st[:, 2].unsqueeze(2).broadcast_to([P, R, P]), ALU.mult))
                for q in range(4):
                    part = sq[:, q * H4:(q + 1) * H4]
                    gain = nc.vector.tensor_tensor(part, part, g[:].unsqueeze(1).broadcast_to([P, H4, P]), ALU.mult)
                    if gate is None:
                        gain.then_inc(ready, 1)
                    else:
                        ch.link(gain)
                        nc.vector.tensor_tensor(part, part, gate[:, q * H4:(q + 1) * H4], ALU.mult).then_inc(ready, 1)

            @block.scalar
            def _(act):
                act.wait_ge(squared, 1)
                nc.scalar.activation(st[:, 1], st[:, 0], ACT.Sqrt, scale=1.0 / P, bias=core.eps[:]).then_inc(rooted, 1)

            @block.sync
            def _(sp):
                per = TT // 4
                for q in range(4):
                    sp.wait_ge(ready, q + 1)
                    sp.dma_start(dst[q * per * P:(q + 1) * per * P, :].rearrange("(t p) n -> p t n", p=P),
                                 sq[:, q * H4:(q + 1) * H4].rearrange("p (t h) d -> p t (h d)", h=4)) \
                        .then_inc(stored, 16)
                sp.wait_ge(stored, 64)


def diff_prepare(core, inp, proj, qT, kT, v, lam4, lam, neglam, g, CT, KT):
    nc = core.nc
    W = DA_H * 2 * DA_DIM
    x_in = [core.sem(f"dap_x_in{b}") for b in range(2)]
    v_in = core.sem("dap_v_in")
    small_in = core.sem("dap_small_in")
    rot = core.sem("dap_rotated")
    rot_pool = core.sem("dap_rotated_pool")
    own = core.sem("dap_dve")
    turned = core.sem("dap_turned")
    q_copied = core.sem("dap_q_copied")
    k_copied = core.sem("dap_k_copied")
    lam_ready = core.sem("dap_lam_ready")
    lam_exp = core.sem("dap_lam_exp")
    lam_sum = core.sem("dap_lam_sum")
    lam_wide = core.sem("dap_lam_wide")
    with ExitStack() as ctx:
        sb = lambda n, s, d=F32: ctx.enter_context(nc.sbuf_tensor("dap_" + n, s, d))
        x = sb("x", [P, 2, 2 * W])
        r = sb("r", [P, 2, 2 * W])
        t = sb("t", [P, 2, 2 * W])
        cs = sb("cs", [P, TT, 2, 32])
        junk = sb("junk", [1, 2, DA_DIM])
        ps = ctx.enter_context(nc.psum_tensor("dap_ps", [P, 2, 2 * BANK], F32))
        psl = ctx.enter_context(nc.psum_tensor("dap_psl", [P, BANK], F32))
        with nc.Block() as block:

            @block.sync
            def _(sp):
                sp.dma_start(cs[:, :, 0], inp["rope_cos"].rearrange("(t p) f -> p t f", p=P)).then_inc(small_in, 16)
                sp.dma_start(cs[:, :, 1], inp["rope_sin"].rearrange("(t p) f -> p t f", p=P)).then_inc(small_in, 16)
                sp.dma_start(lam4[:], inp["da_lambda"]).then_inc(small_in, 16)
                sp.dma_start(g[:], inp["da_subln_g"][0].partition_broadcast(P)).then_inc(small_in, 16)
                for i in range(KT):
                    if i >= 2:
                        sp.wait_ge(turned, i - 1)
                    lo = W if i < CT else 0
                    sp.dma_start(x[:, i % 2, lo:2 * W], proj[i * P:(i + 1) * P, lo:2 * W]).then_inc(x_in[i % 2], 16)
                sp.dma_start(v[:], proj[:, 2 * W:3 * W].rearrange("(t p) n -> p t n", p=P)).then_inc(v_in, 16)
                sp.wait_ge(v_in, 16)

            def views(buf, i):
                return buf[:, i % 2].rearrange("p (g r f) -> p g r f", r=2, f=16)

            def table(i, which):
                return cs[:, i - CT, which].rearrange("p (a f) -> p a f", a=2)

            @block.gpsimd
            def _(pool):
                pool.wait_ge(small_in, 64)
                for i in range(CT, KT):
                    pool.wait_ge(x_in[i % 2], 16 * (i // 2 + 1))
                    if i >= CT + 2:
                        pool.wait_ge(rot, i - CT - 1)
                    a, d = views(x, i), views(t, i)
                    for half in range(2):
                        for ax in range(2):
                            last = nc.gpsimd.tensor_tensor(
                                d[:, ax::2, half, :], a[:, ax::2, 1 - half, :],
                                table(i, 1)[:, ax:ax + 1, :].broadcast_to([P, 2 * W // 64, 16]), ALU.mult)
                    last.then_inc(rot_pool, 1)

            @block.vector
            def _(dve):
                ch = Chain(dve, own)
                dve.wait_ge(small_in, 64)
                for j in range(2):
                    last = nc.vector.tensor_tensor_reduce(junk[:, j], lam4[:, 2 * j], lam4[:, 2 * j + 1], 1.0, 0.0,
                                                          ALU.mult, ALU.add, lam[:, j:j + 1])
                last.then_inc(lam_sum, 1)
                dve.wait_ge(lam_exp, 1)
                ch.link(nc.vector.tensor_tensor(lam[:, 4:5], lam[:, 3:4], lam[:, 2:3], ALU.subtract))
                nc.vector.tensor_scalar(lam[:, 5:6], lam[:, 4:5], -LAMBDA_INIT, None, ALU.add).then_inc(lam_ready, 1)
                dve.wait_ge(lam_wide, 1)
                ch.mark(nc.vector.tensor_copy(neglam[:], psl[:, 0:1]))
                ch.link(nc.vector.tensor_scalar(g[:], g[:], 1.0 - LAMBDA_INIT, None, ALU.mult))

                def k_out(i):
                    dve.wait_ge(turned, i + 1)
                    nc.vector.tensor_copy(kT[:, :, i * P:(i + 1) * P],
                                          ps[:, i % 2, BANK:2 * BANK].rearrange("p (h n) -> p h n", h=DA_H)) \
                        .then_inc(k_copied, 1)

                for i in range(KT):
                    if i >= CT:
                        dve.wait_ge(x_in[i % 2], 16 * (i // 2 + 1))
                        if i >= CT + 2:
                            dve.wait_ge(turned, i - 1)
                        a, d, tt = views(x, i), views(r, i), views(t, i)
                        for half in range(2):
                            for ax in range(2):
                                ch.mark(nc.vector.tensor_tensor(
                                    d[:, ax::2, half, :], a[:, ax::2, half, :],
                                    table(i, 0)[:, ax:ax + 1, :].broadcast_to([P, 2 * W // 64, 16]), ALU.mult))
                        ch.settle()
                        dve.wait_ge(rot_pool, i - CT + 1)
                        nc.vector.tensor_tensor(d[:, :, 0], d[:, :, 0], tt[:, :, 0], ALU.subtract)
                        nc.vector.tensor_tensor(d[:, :, 1], d[:, :, 1], tt[:, :, 1], ALU.add).then_inc(rot, 1)
                    if i >= 1:
                        k_out(i - 1)
                k_out(KT - 1)
                dve.wait_ge(k_copied, KT)

            @block.scalar
            def _(act):
                act.wait_ge(lam_sum, 1)
                nc.scalar.activation(lam[:, 2:4], lam[:, 0:2], ACT.Exp).then_inc(lam_exp, 1)
                for i in range(CT, KT):
                    act.wait_ge(turned, i + 1)
                    nc.scalar.copy(qT[:, :, (i - CT) * P:(i - CT + 1) * P],
                                   ps[:, i % 2, 0:BANK].rearrange("p (h n) -> p h n", h=DA_H)).then_inc(q_copied, 1)
                act.wait_ge(q_copied, TT)

            @block.tensor
            def _(pe):
                pe.wait_ge(lam_ready, 1)
                nc.tensor.matmul(psl[:, 0:1], core.ones[0:1, :], lam[:, 5:6], start=True, stop=True).then_inc(lam_wide, 1)
                for i in range(KT):
                    if i >= 2:
                        pe.wait_ge(k_copied, i - 1)
                    if i >= CT + 2:
                        pe.wait_ge(q_copied, i - CT - 1)
                    if i < CT:
                        pe.wait_ge(x_in[i % 2], 16 * (i // 2 + 1))
                        src = x
                    else:
                        pe.wait_ge(rot, i - CT + 1)
                        src = r
                    for c in range(DA_H if i < CT else 0, 2 * DA_H):
                        last = nc.tensor.transpose(ps[:, i % 2, c * P:(c + 1) * P], src[:, i % 2, c * P:(c + 1) * P],
                                                   core.ident[:])
                    last.then_inc(turned, 1)


def rope_tables():
    n_freq, grid = 16, 64
    inv = np.power(np.float32(10000.0), -np.arange(n_freq, dtype=np.float32) / n_freq).astype(np.float32)
    tok = np.arange(T)
    pos = np.stack([tok // grid, tok % grid], -1).astype(np.float32)
    ang = (pos[:, :, None] * inv).astype(np.float32).reshape(T, 2 * n_freq)
    return np.cos(ang).astype(np.float32), np.sin(ang).astype(np.float32)


GLA_H, GLA_K, GLA_V, GLA_R, GLA_C = 4, 64, 128, 16, 64
GLA_TAU = 16.0


def gated_linear_attention(core, inp, proj, mix):
    nc = core.nc
    KT = proj.shape[0] // P
    CT = KT - TT
    C0 = 3 * 512
    HK = GLA_H * GLA_K
    HV = GLA_H * GLA_V
    with ExitStack() as ctx:
        sb = lambda n, s, d=F32: ctx.enter_context(nc.sbuf_tensor("gla_" + n, s, d))
        qd = sb("q_dec", [P, TT, 2, 2, P])
        ki = sb("k_inv", [P, TT, 2, 2, P])
        state = sb("state", [P, KT, 2, 2, 2, GLA_V])
        decay = sb("decay", [P, KT, 2, 2, 2])
        v = sb("v", [P, KT, HV])
        g = sb("gain", [P, GLA_V])

        lr_in = [core.sem(f"gla_x_in{b}") for b in range(2)]
        small_in = core.sem("gla_small_in")
        v_in = core.sem("gla_v_in")
        prepared = core.sem("gla_prepared")
        own = core.sem("gla_dve")
        acts = core.sem("gla_act")
        lr_turned = core.sem("gla_lr_turned")
        lr_copied = core.sem("gla_lr_copied")
        z_done = core.sem("gla_z_done")
        ln_done = core.sem("gla_ln_done")
        g_ready = core.sem("gla_g_ready")
        b_done = core.sem("gla_b_done")
        exp_done = core.sem("gla_exp_done")
        ke_ready = core.sem("gla_ke_ready")
        qk_used = core.sem("gla_qk_used")
        ds_done = core.sem("gla_ds_done")
        ds_copied = core.sem("gla_ds_copied")
        with ExitStack() as c2:
            s2 = lambda n, s, d=F32: c2.enter_context(nc.sbuf_tensor("gla_" + n, s, d))
            pt = lambda n: c2.enter_context(nc.psum_tensor("gla_" + n, [P, BANK], F32))
            qk = s2("qk", [P, 2, 2 * HK])
            lr = s2("lr", [P, 2, 2 * GLA_R])
            lrT = s2("lrT", [GLA_R + 1, 2, P])
            w2 = s2("w2", [GLA_R + 1, 2, HK])
            after = s2("after", [P, 2, P])
            az = s2("az", [P, 2 * HK])
            gates = s2("gates", [P, 2 * HK])
            eb = s2("eb", [P, 2, 2, P])
            enb = s2("enb", [P, 2, 2, P])
            ek = s2("ek", [P, 2, HK])
            ke = s2("ke", [P, 2, HK])
            ps_l, ps_z, ps_b, ps_k, ps_q = pt("ps_l"), pt("ps_z"), pt("ps_b"), pt("ps_k"), pt("ps_q")
            ps_s = c2.enter_context(nc.psum_tensor("gla_ps_s", [P, 2, 2, 2, GLA_V], F32))
            with nc.Block() as block:

                @block.sync
                def _(sp):
                    sp.wait_ge(prepared, 1)
                    sp.dma_start(w2[0:GLA_R], inp["gla_gate_w2"][0].rearrange("d r n -> r d n")).then_inc(small_in, 16)
                    sp.dma_start(w2[GLA_R:GLA_R + 1], inp["gla_gate_b"]).then_inc(small_in, 16)
                    sp.dma_start(g[:], inp["gla_norm_g"][0].partition_broadcast(P)).then_inc(small_in, 16)
                    for i in range(KT):
                        if i >= 2:
                            sp.wait_ge(ke_ready, i - 1)
                            sp.wait_ge(lr_turned, i - 1)
                        rows = proj[i * P:(i + 1) * P]
                        sp.dma_start(qk[:, i % 2], rows[:, C0:C0 + 2 * HK]).then_inc(lr_in[i % 2], 16)
                        sp.dma_start(lr[:, i % 2], rows[:, C0 + 2 * HK + 2 * HV:C0 + 2 * HK + 2 * HV + 2 * GLA_R]) \
                            .then_inc(lr_in[i % 2], 16)
                        if i == 0:
                            sp.dma_start(v[:], proj[:, C0 + 2 * HK:C0 + 2 * HK + HV].rearrange("(t p) n -> p t n", p=P)) \
                                .then_inc(v_in, 16)
                    sp.wait_ge(small_in, 48)

                @block.gpsimd
                def _(pool):
                    nc.gpsimd.memset(lrT[:], 1.0)
                    nc.gpsimd.memset(w2[:], 0.0)
                    nc.gpsimd.tensor_tensor(after[:, 0], core.chunk_suffix[:], core.ident[:], ALU.subtract)
                    nc.gpsimd.tensor_tensor(after[:, 1], core.chunk_incl[:], core.ident[:], ALU.subtract) \
                        .then_inc(prepared, 1)

                @block.tensor
                def _(pe):
                    pe.wait_ge(small_in, 48)
                    pe.wait_ge(v_in, 16)
                    for i in range(KT):
                        b = i % 2
                        pe.wait_ge(lr_in[b], 32 * (i // 2 + 1))
                        if i >= 1:
                            pe.wait_ge(qk_used, i)
                        for d in range(2):
                            nc.tensor.transpose(ps_l[0:GLA_R, d * P:(d + 1) * P], lr[:, b, d * GLA_R:(d + 1) * GLA_R],
                                                core.ident[:])
                        for c in range(4):
                            last = nc.tensor.transpose(ps_q[:, c * P:(c + 1) * P], qk[:, b, c * P:(c + 1) * P],
                                                       core.ident[:])
                        last.then_inc(lr_turned, 1)
                        pe.wait_ge(lr_copied, i + 1)
                        for d in range(2):
                            last = nc.tensor.matmul(ps_z[:, d * HK:(d + 1) * HK], lrT[:, d, :], w2[:, d, :],
                                                    start=True, stop=True)
                        last.then_inc(z_done, 1)
                        pe.wait_ge(g_ready, i + 1)
                        for d, incl in enumerate((core.chunk_incl, core.chunk_suffix)):
                            for c in range(2):
                                nc.tensor.matmul(ps_b[:, (2 * d + c) * P:(2 * d + c + 1) * P],
                                                 gates[:, d * HK + c * P:d * HK + (c + 1) * P], incl[:],
                                                 start=True, stop=True)
                            last = nc.tensor.matmul(ps_k[:, d * HK:(d + 1) * HK], after[:, d],
                                                    gates[:, d * HK:(d + 1) * HK], start=True, stop=True)
                        last.then_inc(b_done, 1)
                        pe.wait_ge(ke_ready, i + 1)
                        if i >= 1:
                            pe.wait_ge(ds_copied, i)
                        for s in range(2):
                            rows = slice(64 * s, 64 * s + 64)
                            for d in range(2):
                                for h in range(GLA_H):
                                    r = 64 * (h % 2)
                                    last = nc.tensor.matmul(ps_s[r:r + 64, s, d, h // 2, :],
                                                            ke[rows, d, h * GLA_K:(h + 1) * GLA_K],
                                                            v[rows, i, h * GLA_V:(h + 1) * GLA_V], start=True, stop=True)
                        last.then_inc(ds_done, 1)

                @block.scalar
                def _(act):
                    ch = Chain(act, acts)
                    for i in range(KT):
                        act.wait_ge(z_done, i + 1)
                        ch.link(nc.scalar.activation(az[:], ps_z[:], ACT.Abs))
                        ch.link(nc.scalar.activation(az[:], az[:], ACT.Exp, scale=-1.0))
                        nc.scalar.activation(az[:], az[:], ACT.Ln, bias=1.0).then_inc(ln_done, 1)
                        act.wait_ge(b_done, i + 1)
                        if i >= 1:
                            act.wait_ge(qk_used, i)
                        flat = "p d c t -> p (d c t)"
                        nc.scalar.activation(eb[:].rearrange(flat), ps_b[:], ACT.Exp, scale=1.0 / GLA_TAU)
                        nc.scalar.activation(enb[:].rearrange(flat), ps_b[:], ACT.Exp, scale=-1.0 / GLA_TAU)
                        nc.scalar.activation(ek[:].rearrange("p d n -> p (d n)"), ps_k[:], ACT.Exp,
                                             scale=1.0 / GLA_TAU).then_inc(exp_done, 1)

                @block.vector
                def _(dve):
                    ch = Chain(dve, own)
                    dve.wait_ge(prepared, 1)
                    for i in range(KT):
                        b = i % 2
                        dve.wait_ge(lr_turned, i + 1)
                        nc.vector.tensor_copy(lrT[0:GLA_R].rearrange("r d t -> r (d t)"), ps_l[0:GLA_R, 0:2 * P]) \
                            .then_inc(lr_copied, 1)
                        dve.wait_ge(ln_done, i + 1)
                        nc.vector.scalar_tensor_tensor(gates[:], ps_z[:], 0.0, az[:], ALU.min, ALU.subtract) \
                            .then_inc(g_ready, 1)
                        dve.wait_ge(exp_done, i + 1)
                        if i >= 1:
                            dve.wait_ge(ds_done, i)
                        dve.wait_ge(lr_in[b], 32 * (i // 2 + 1))
                        k_rows = qk[:, b, HK:2 * HK].unsqueeze(1).broadcast_to([P, 2, HK])
                        nc.vector.tensor_tensor(ke[:], k_rows, ek[:], ALU.mult).then_inc(ke_ready, 1)
                        if i >= CT:
                            for d in range(2):
                                nc.vector.scalar_tensor_tensor(qd[:, i - CT, d], ps_q[:, 0:2 * P].rearrange("p (c t) -> p c t", c=2),
                                                               GLA_K ** -0.5, eb[:, d], ALU.mult, ALU.mult)
                                nc.vector.tensor_tensor(ki[:, i - CT, d], ps_q[:, 2 * P:4 * P].rearrange("p (c t) -> p c t", c=2),
                                                        enb[:, d], ALU.mult)
                        nc.vector.tensor_copy(decay[:, i, :, 0].rearrange("p s c -> p c s"), eb[:, 0, :, 63::64])
                        nc.vector.tensor_copy(decay[:, i, :, 1].rearrange("p s c -> p c s"), eb[:, 1, :, 0::64]) \
                            .then_inc(qk_used, 1)
                        dve.wait_ge(ds_done, i + 1)
                        for s in range(2):
                            last = nc.vector.tensor_copy(state[:, i, s], ps_s[:, s])
                        last.then_inc(ds_copied, 1)
                    dve.wait_ge(ds_copied, KT)
                    order_f = [(t, s) for t in range(KT) for s in range(2)]
                    order_b = [(t, s) for t in [*range(CT)][::-1] + [*range(CT, KT)][::-1] for s in (1, 0)]
                    dve.wait_ge(qk_used, KT)
                    for n in range(1, 2 * KT):
                        for d, order in enumerate((order_f, order_b)):
                            (t0, s0), (t1, s1) = order[n - 1], order[n]
                            for c in range(2):
                                ch.mark(nc.vector.scalar_tensor_tensor(
                                    state[:, t1, s1, d, c], state[:, t0, s0, d, c], decay[:, t1, s1, d, c:c + 1],
                                    state[:, t1, s1, d, c], ALU.mult, ALU.add))
                        ch.settle()

        gr_in = core.sem("gla_gr_in")
        silu_done = core.sem("gla_silu_done")
        sc_done = core.sem("gla_scores_done")
        masked = core.sem("gla_masked")
        o_done = core.sem("gla_o_done")
        o_copied = core.sem("gla_o_copied")
        order_f = [(t, s) for t in range(KT) for s in range(2)]
        order_b = [(t, s) for t in [*range(CT)][::-1] + [*range(CT, KT)][::-1] for s in (1, 0)]
        o = sb("o", [P, TT, GLA_H, GLA_V])
        gr = sb("gr", [P, TT * GLA_H, GLA_V])
        with ExitStack() as c2:
            sT = c2.enter_context(nc.sbuf_tensor("gla_sT", [P, 2, 2, 2, 2, P], F32))
            ps_c = c2.enter_context(nc.psum_tensor("gla_ps_c", [P, 2, 2, 2, 2, P], F32))
            ps_o = c2.enter_context(nc.psum_tensor("gla_ps_o", [P, 2, 2, BANK], F32))
            with nc.Block() as block:

                @block.sync
                def _(sp):
                    lo = C0 + 2 * HK + HV
                    sp.dma_start(gr[:].rearrange("p (t h) d -> p t (h d)", h=GLA_H),
                                 proj[CT * P:, lo:lo + HV].rearrange("(t p) n -> p t n", p=P)).then_inc(gr_in, 16)

                @block.tensor
                def _(pe):
                    def scores(i):
                        if i >= 2:
                            pe.wait_ge(masked, i - 1)
                        for d in range(2):
                            for h in range(GLA_H):
                                rows = slice(64 * (h % 2), 64 * (h % 2) + 64)
                                last = nc.tensor.matmul(ps_c[:, i % 2, h % 2, d, h // 2], ki[rows, i, d, h // 2, :],
                                                        qd[rows, i, d, h // 2, :], start=True, stop=True)
                        last.then_inc(sc_done, 1)

                    def outputs(i):
                        pe.wait_ge(masked, i + 1)
                        if i >= 2:
                            pe.wait_ge(o_copied, i - 1)
                        for h in range(GLA_H):
                            rows = slice(64 * (h % 2), 64 * (h % 2) + 64)
                            out_at = slice(h // 2 * GLA_V, (h // 2 + 1) * GLA_V)
                            for d in range(2):
                                nc.tensor.matmul(ps_o[:, i % 2, h % 2, out_at], sT[:, i % 2, h % 2, d, h // 2, :],
                                                 v[:, CT + i, h * GLA_V:(h + 1) * GLA_V], start=(d == 0), stop=False)
                            for d, order in enumerate((order_f, order_b)):
                                for s in range(2):
                                    t0, s0 = order[order.index((CT + i, s)) - 1]
                                    last = nc.tensor.matmul(ps_o[64 * s:64 * s + 64, i % 2, h % 2, out_at],
                                                            qd[rows, i, d, h // 2, 64 * s:64 * s + 64],
                                                            state[rows, t0, s0, d, h // 2, :], start=False, stop=(d == 1))
                        last.then_inc(o_done, 1)

                    for i in range(TT + 1):
                        if i < TT:
                            scores(i)
                        if i >= 1:
                            outputs(i - 1)

                @block.vector
                def _(dve):
                    for i in range(TT):
                        dve.wait_ge(sc_done, i + 1)
                        if i >= 2:
                            dve.wait_ge(o_done, i - 1)
                        for d, m in enumerate((core.chunk_incl, core.chunk_suffix)):
                            for odd in range(2):
                                last = nc.vector.tensor_tensor(sT[:, i % 2, odd, d], ps_c[:, i % 2, odd, d],
                                                               m[:].unsqueeze(1).broadcast_to([P, 2, P]), ALU.mult)
                        last.then_inc(masked, 1)

                @block.scalar
                def _(act):
                    act.wait_ge(gr_in, 16)
                    nc.scalar.activation(gr[:], gr[:], ACT.Silu).then_inc(silu_done, 1)
                    for i in range(TT):
                        act.wait_ge(o_done, i + 1)
                        nc.scalar.copy(o[:, i].rearrange("p (c x) d -> p x c d", x=2),
                                       ps_o[:, i % 2, :, 0:2 * GLA_V].rearrange("p x (c d) -> p x c d", c=2)) \
                            .then_inc(o_copied, 1)
                    act.wait_ge(silu_done, 1)
                    act.wait_ge(o_copied, TT)
        head_norm(core, "gla_norm", o, g, mix[:, 512:1024], gr)


def turn_rows(core, name, rows, hT, kc):
    nc = core.nc
    n = rows.shape[0] // P
    loaded = [core.sem(f"{name}_loaded{b}") for b in range(2)]
    turned = core.sem(f"{name}_turned")
    high_done = core.sem(f"{name}_high_done")
    low_done = core.sem(f"{name}_low_done")
    high, low = hT
    banks = -(-kc // 4)
    with ExitStack() as ctx:
        xt = ctx.enter_context(nc.sbuf_tensor(f"{name}_xt", [P, 2, kc * P], F32))
        ps = ctx.enter_context(nc.psum_tensor(f"{name}_ps", [P, 2, banks * BANK], F32))
        with nc.Block() as block:

            @block.sync
            def _(sp):
                for i in range(n):
                    if i >= 2:
                        sp.wait_ge(turned, i - 1)
                    sp.dma_start(xt[:, i % 2], rows[i * P:(i + 1) * P, :]).then_inc(loaded[i % 2], 16)

            @block.tensor
            def _(pe):
                for i in range(n):
                    pe.wait_ge(loaded[i % 2], 16 * (i // 2 + 1))
                    if i >= 2:
                        pe.wait_ge(low_done, i - 1)
                    for k in range(kc):
                        last = nc.tensor.transpose(ps[:, i % 2, k * P:(k + 1) * P], xt[:, i % 2, k * P:(k + 1) * P],
                                                   core.ident[:])
                    last.then_inc(turned, 1)

            def tile(i):
                return slice(i * P, (i + 1) * P), ps[:, i % 2, 0:kc * P].rearrange("p (k t) -> p k t", t=P)

            @block.scalar
            def _(act):
                for i in range(n):
                    act.wait_ge(turned, i + 1)
                    toks, x = tile(i)
                    nc.scalar.copy(high[:, :, toks], x).then_inc(high_done, 1)
                act.wait_ge(high_done, n)

            @block.vector
            def _(dve):
                for i in range(n):
                    dve.wait_ge(high_done, i + 1)
                    toks, x = tile(i)
                    low_part(nc, low[:, :, toks], x, high[:, :, toks]).then_inc(low_done, 1)
                dve.wait_ge(low_done, n)


def residual_product(core, name, hT, w, x, gate, out):
    nc = core.nc
    wv = w.rearrange("(k p) n -> p k n", p=P)
    w_in = [core.sem(f"{name}_w_in{b}") for b in range(2)]
    x_in = [core.sem(f"{name}_x_in{b}") for b in range(2)]
    done = core.sem(f"{name}_done")
    w_high = core.sem(f"{name}_w_high")
    w_split = core.sem(f"{name}_w_split")
    high, low = hT
    own = core.sem(f"{name}_dve")
    added = core.sem(f"{name}_added")
    stored = [core.sem(f"{name}_stored{b}") for b in range(2)]
    with ExitStack() as ctx:
        raw = ctx.enter_context(nc.sbuf_tensor(f"{name}_w", [P, 2, D], F32))
        w_h, w_l = pair(core, ctx, f"{name}_w", [P, KD, D])
        xt = ctx.enter_context(nc.sbuf_tensor(f"{name}_x", [P, 2, D], F32))
        yt = ctx.enter_context(nc.sbuf_tensor(f"{name}_y", [P, 2, D], F32))
        ps = ctx.enter_context(nc.psum_tensor(f"{name}_ps", [P, 2, 2 * BANK], F32))
        with nc.Block() as block:

            @block.sync
            def _(sp):
                for k in range(KD):
                    if k >= 2:
                        sp.wait_ge(w_split, k - 1)
                    sp.dma_start(raw[:, k % 2], wv[:, k]).then_inc(w_in[k % 2], 16)
                for i in range(TT):
                    if i >= 2:
                        sp.wait_ge(added, i - 1)
                    sp.dma_start(xt[:, i % 2], x[i * P:(i + 1) * P, :]).then_inc(x_in[i % 2], 16)

            @block.tensor
            def _(pe):
                for i in range(TT):
                    if i == 0:
                        pe.wait_ge(w_split, KD)
                    if i >= 2:
                        pe.wait_ge(added, i - 1)
                    toks = slice(i * P, (i + 1) * P)
                    for h in range(2):
                        cols = slice(h * BANK, (h + 1) * BANK)
                        last = split_matmuls(nc, ps[:, i % 2, cols],
                                             [(high[:, k, toks], low[:, k, toks], w_h[:, k, cols], w_l[:, k, cols])
                                              for k in range(KD)])
                    last.then_inc(done, 1)

            @block.scalar
            def _(act):
                for k in range(KD):
                    act.wait_ge(w_in[k % 2], 16 * (k // 2 + 1))
                    nc.scalar.copy(w_h[:, k], raw[:, k % 2]).then_inc(w_high, 1)

            @block.vector
            def _(dve):
                for k in range(KD):
                    dve.wait_ge(w_high, k + 1)
                    low_part(nc, w_l[:, k], raw[:, k % 2], w_h[:, k]).then_inc(w_split, 1)
                ch = Chain(dve, own)
                for i in range(TT):
                    dve.wait_ge(done, i + 1)
                    dve.wait_ge(x_in[i % 2], 16 * (i // 2 + 1))
                    if i >= 2:
                        dve.wait_ge(stored[i % 2], 16 * (i // 2))
                    y = ps[:, i % 2]
                    if gate is not None:
                        ch.link(nc.vector.tensor_tensor(yt[:, i % 2], y, gate, ALU.mult))
                        y = yt[:, i % 2]
                    nc.vector.tensor_tensor(yt[:, i % 2], y, xt[:, i % 2], ALU.add).then_inc(added, 1)

            @block.gpsimd
            def _(pool):
                for i in range(TT):
                    pool.wait_ge(added, i + 1)
                    pool.dma_start(out[i * P:(i + 1) * P, :], yt[:, i % 2]).then_inc(stored[i % 2], 16)
                for b in range(2):
                    pool.wait_ge(stored[b], 16 * TT // 2)


EPG = 8
SLOTS = P
OVER = 2 * T // (SLOTS + 1)


class Routing:

    def __init__(self, core, name, E):
        self.E, self.NB = E, E + OVER
        self.dest = core.ctx_keep(f"{name}_dest", [P, TT, 2], I32)
        self.weight = core.ctx_keep(f"{name}_weight", [P, TT, 2], F32)
        self.row_tok = core.ctx_keep(f"{name}_row_tok", [P, self.NB], I32)
        self.block_e = core.ctx_keep(f"{name}_block_e", [1, self.NB], I32)
        self.used = core.ctx_keep(f"{name}_used", [1, 1], I32)


def route(core, name, hT, wg, we, bg, be, rt, y_rows):
    nc = core.nc
    G, E, NB = wg.shape[1], rt.E, rt.NB
    GE = G + E
    small_in = core.sem(f"{name}_small_in")
    idx_ready = core.sem(f"{name}_idx_ready")
    zero_ready = core.sem(f"{name}_zero_ready")
    zeros_stored = core.sem(f"{name}_zeros_stored")
    logits_done = core.sem(f"{name}_logits_done")
    own = core.sem(f"{name}_dve")
    shifted = core.sem(f"{name}_shifted")
    exp_done = core.sem(f"{name}_exp_done")
    picks_ready = core.sem(f"{name}_picks_ready")
    ranks_done = core.sem(f"{name}_ranks_done")
    hot_ready = core.sem(f"{name}_hot_ready")
    toks_done = core.sem(f"{name}_toks_done")
    with ExitStack() as ctx:
        sb = lambda n, s, d=F32: ctx.enter_context(nc.sbuf_tensor(f"{name}_{n}", s, d))
        w = sb("w", [P, KD, GE])
        bias = sb("bias", [P, GE])
        idx = sb("idx", [P, P])
        zero = sb("zero", [P, D])
        tok = sb("tok", [P, TT])
        thr = sb("thr", [P, 7])
        first = sb("first", [P, E])
        beyond = sb("beyond", [P, E])
        lg = sb("lg", [P, TT, GE])
        gp = sb("gp", [P, TT, 8])
        gm, em = sb("gm", [P, TT, 8]), sb("em", [P, TT, 8])
        gi, ei = sb("gi", [P, TT, 8], U32), sb("ei", [P, TT, 8], U32)
        gif, eif = sb("gif", [P, TT]), sb("eif", [P, TT, 2])
        gsel = sb("gsel", [P, TT, G])
        gx = sb("gx", [P, TT, G])
        gsum = sb("gsum", [P, TT])
        prod = sb("prod", [P, TT, G, EPG])
        ein = sb("ein", [P, TT, EPG])
        dd = sb("dd", [P, TT, 4])
        picks = sb("picks", [P, TT, 2, E])
        both = sb("both", [P, TT, E])
        rank = sb("rank", [P, TT, E])
        cnt = sb("cnt", [P, 6, E])
        cmp = sb("cmp", [P, E, 7])
        place = sb("place", [P, TT, E])
        pp = sb("pp", [P, TT, 2, E])
        destf = sb("destf", [P, TT, 2])
        blk, slot = sb("blk", [P, TT * 2], I32), sb("slot", [P, TT * 2], I32)
        blkf, slotf = sb("blkf", [P, TT * 2]), sb("slotf", [P, TT * 2])
        hot_s = sb("hot_s", [P, TT * 2, P])
        hot_b = sb("hot_b", [P, TT * 2, NB])
        bcmp = sb("bcmp", [1, OVER, E])
        bef = sb("bef", [1, NB])
        ps_l = ctx.enter_context(nc.psum_tensor(f"{name}_ps_l", [P, 2, BANK], F32))
        ps_r = ctx.enter_context(nc.psum_tensor(f"{name}_ps_r", [P, TT, E], F32))
        ps_c = ctx.enter_context(nc.psum_tensor(f"{name}_ps_c", [P, BANK], F32))
        ps_t = ctx.enter_context(nc.psum_tensor(f"{name}_ps_t", [P, BANK], F32))
        half = TT // 2
        with nc.Block() as block:

            @block.sync
            def _(sp):
                sp.dma_start(w[:, :, 0:G], wg.rearrange("(k p) n -> p k n", p=P)).then_inc(small_in, 16)
                sp.dma_start(w[:, :, G:GE], we.rearrange("(k p) n -> p k n", p=P)).then_inc(small_in, 16)
                sp.dma_start(bias[:, 0:G], bg.partition_broadcast(P)).then_inc(small_in, 16)
                sp.dma_start(bias[:, G:GE], be.partition_broadcast(P)).then_inc(small_in, 16)
                sp.wait_ge(zero_ready, 1)
                sp.dma_start(y_rows[E * SLOTS:, :].rearrange("(j p) n -> p j n", p=SLOTS),
                             zero[:].unsqueeze(1).broadcast_to([P, OVER, D])).then_inc(zeros_stored, 16)
                sp.wait_ge(zeros_stored, 16)

            @block.gpsimd
            def _(pool):
                def iota(out, pattern, base, per_partition):
                    return nc.gpsimd.iota(out, pattern, base=base, channel_multiplier=per_partition,
                                          allow_small_or_imprecise_dtypes=True)

                nc.gpsimd.memset(zero[:], 0.0).then_inc(zero_ready, 1)
                iota(idx[:], [[1, P]], 0, 0)
                iota(tok[:], [[P, TT]], 0, 1)
                iota(thr[:], [[SLOTS, 7]], SLOTS, 0)
                iota(first[:], [[SLOTS, E]], 0, 0)
                iota(beyond[:], [[-SLOTS, E]], SLOTS * (E - 1), 0)
                nc.gpsimd.memset(gp[:], -3.0e38).then_inc(idx_ready, 1)

            @block.tensor
            def _(pe):
                pe.wait_ge(small_in, 64)
                for i in range(TT):
                    for k in range(KD):
                        last = nc.tensor.matmul(ps_l[:, i // half, (i % half) * GE:(i % half + 1) * GE],
                                                hT[:, k, i * P:(i + 1) * P], w[:, k, :], start=(k == 0), stop=(k == KD - 1))
                last.then_inc(logits_done, 1)
                pe.wait_ge(picks_ready, 1)
                for i in range(TT):
                    for j in range(i):
                        nc.tensor.matmul(ps_r[:, i, :], core.ones[:], both[:, j, :], start=(j == 0), stop=False)
                    nc.tensor.matmul(ps_r[:, i, :], core.before[:], both[:, i, :], start=(i == 0), stop=True)
                for j in range(TT):
                    last = nc.tensor.matmul(ps_c[:, 0:E], core.ones[:], both[:, j, :], start=(j == 0), stop=(j == TT - 1))
                last.then_inc(ranks_done, 1)
                pe.wait_ge(hot_ready, 1)
                for n in range(2 * TT):
                    last = nc.tensor.matmul(ps_t[:, 0:NB], hot_s[:, n, :], hot_b[:, n, :], start=(n == 0),
                                            stop=(n == 2 * TT - 1))
                last.then_inc(toks_done, 1)

            @block.scalar
            def _(act):
                act.wait_ge(shifted, 1)
                nc.scalar.activation(gx[:], gx[:], ACT.Exp).then_inc(exp_done, 1)
                act.wait_ge(shifted, 2)
                nc.scalar.activation(dd[:, :, 1], dd[:, :, 0], ACT.Exp).then_inc(exp_done, 1)

            @block.vector
            def _(dve):
                ch = Chain(dve, own)
                V = nc.vector
                wide = lambda a, n: a.unsqueeze(2).broadcast_to([P, TT, n])
                dve.wait_ge(logits_done, 1)
                for x in range(2):
                    ch.mark(V.tensor_tensor(lg[:, x * half:(x + 1) * half],
                                            ps_l[:, x, 0:half * GE].rearrange("p (t e) -> p t e", e=GE),
                                            bias[:].unsqueeze(1).broadcast_to([P, half, GE]), ALU.add))
                dve.wait_ge(idx_ready, 1)
                ch.settle()
                ch.link(V.tensor_copy(gp[:, :, 0:G], lg[:, :, 0:G]))
                for i in range(TT):
                    ch.mark(V.max(gm[:, i], gp[:, i]))
                ch.settle()
                for i in range(TT):
                    ch.mark(V.max_index(gi[:, i], gm[:, i], gp[:, i]))
                V.tensor_tensor(gx[:], lg[:, :, 0:G], wide(gm[:, :, 0], G), ALU.subtract).then_inc(shifted, 1)
                ch.settle()
                ch.link(V.tensor_copy(gif[:], gi[:, :, 0]))
                ch.link(V.tensor_tensor(gsel[:], idx[:, 0:G].unsqueeze(1).broadcast_to([P, TT, G]), wide(gif[:], G),
                                        ALU.is_equal))
                for i in range(TT):
                    ch.mark(V.tensor_tensor(prod[:, i], lg[:, i, G:GE].rearrange("p (g e) -> p g e", e=EPG),
                                            gsel[:, i].unsqueeze(2).broadcast_to([P, G, EPG]), ALU.mult))
                ch.settle()
                ch.link(V.reduce_sum(ein[:], prod[:].rearrange("p t g e -> p t e g"), AX_X))
                for i in range(TT):
                    ch.mark(V.max(em[:, i], ein[:, i]))
                ch.settle()
                for i in range(TT):
                    ch.mark(V.max_index(ei[:, i], em[:, i], ein[:, i]))
                V.tensor_tensor(dd[:, :, 0], em[:, :, 1], em[:, :, 0], ALU.subtract).then_inc(shifted, 1)
                ch.settle()
                ch.link(V.tensor_copy(eif[:], ei[:, :, 0:2]))
                ch.link(V.scalar_tensor_tensor(eif[:], wide(gif[:], 2), float(EPG), eif[:], ALU.mult, ALU.add))
                for i in range(TT):
                    ch.mark(V.tensor_tensor(picks[:, i], idx[:, 0:E].unsqueeze(1).broadcast_to([P, 2, E]),
                                            eif[:, i].unsqueeze(2).broadcast_to([P, 2, E]), ALU.is_equal))
                ch.settle()
                V.tensor_tensor(both[:], picks[:, :, 0], picks[:, :, 1], ALU.add).then_inc(picks_ready, 1)
                dve.wait_ge(exp_done, 2)
                ch.mark(V.reduce_sum(gsum[:], gx[:], AX_X))
                ch.link(V.tensor_scalar(dd[:, :, 2], dd[:, :, 1], 1.0, None, ALU.add))
                ch.link(V.tensor_tensor(dd[:, :, 3], dd[:, :, 2], gsum[:], ALU.mult))
                ch.link(V.reciprocal(rt.weight[:, :, 0], dd[:, :, 3]))
                ch.mark(V.tensor_tensor(rt.weight[:, :, 1], rt.weight[:, :, 0], dd[:, :, 1], ALU.mult))
                dve.wait_ge(ranks_done, 1)
                ch.mark(V.tensor_copy(rank[:], ps_r[:]))
                ch.link(V.tensor_copy(cnt[:, 0], ps_c[:, 0:E]))
                ch.link(V.tensor_tensor(cmp[:], cnt[:, 0].unsqueeze(2).broadcast_to([P, E, 7]),
                                        thr[:].unsqueeze(1).broadcast_to([P, E, 7]), ALU.is_gt))
                ch.link(V.reduce_sum(cnt[:, 1], cmp[:], AX_X))
                ch.link(V.tensor_tensor_scan(cnt[:, 2], core.ones[:, 0:E], cnt[:, 1], 0.0, ALU.mult, ALU.add))
                ch.link(V.tensor_tensor(cnt[:, 3], cnt[:, 2], cnt[:, 1], ALU.subtract))
                ch.link(V.scalar_tensor_tensor(cnt[:, 4], cnt[:, 3], float(SLOTS), beyond[:], ALU.mult, ALU.add))
                row = lambda a: a.unsqueeze(1).broadcast_to([P, TT, E])
                ch.link(V.scalar_tensor_tensor(place[:], rank[:], float(SLOTS), row(cnt[:, 4]), ALU.is_ge, ALU.mult))
                ch.link(V.tensor_tensor(place[:], place[:], rank[:], ALU.add))
                ch.link(V.tensor_tensor(place[:], place[:], row(first[:]), ALU.add))
                for x in range(2):
                    ch.mark(V.tensor_tensor(pp[:, :, x], picks[:, :, x], place[:], ALU.mult))
                ch.settle()
                ch.link(V.reduce_sum(destf[:], pp[:], AX_X))
                ch.link(V.tensor_copy(rt.dest[:], destf[:]))
                flat = rt.dest[:].rearrange("p t x -> p (t x)")
                ch.mark(V.tensor_scalar(blk[:], flat, 7, None, ALU.logical_shift_right))
                ch.link(V.tensor_scalar(slot[:], flat, SLOTS - 1, None, ALU.bitwise_and))
                ch.mark(V.tensor_copy(blkf[:], blk[:]))
                ch.link(V.tensor_copy(slotf[:], slot[:]))
                ch.mark(V.tensor_tensor(hot_s[:], idx[:].unsqueeze(1).broadcast_to([P, 2 * TT, P]),
                                        slotf[:].unsqueeze(2).broadcast_to([P, 2 * TT, P]), ALU.is_equal))
                ch.link(V.tensor_tensor(hot_b[:], idx[:, 0:NB].unsqueeze(1).broadcast_to([P, 2 * TT, NB]),
                                        blkf[:].unsqueeze(2).broadcast_to([P, 2 * TT, NB]), ALU.is_equal))
                for i in range(TT):
                    last = V.tensor_scalar(hot_b[:, 2 * i:2 * i + 2], hot_b[:, 2 * i:2 * i + 2], tok[:, i:i + 1], None,
                                           ALU.mult)
                last.then_inc(hot_ready, 1)
                ch.mark(V.tensor_copy(bef[:, 0:E], idx[0:1, 0:E]))
                ch.link(V.tensor_tensor(bcmp[:], cnt[0:1, 2].unsqueeze(1).broadcast_to([1, OVER, E]),
                                        idx[0:1, 0:OVER].unsqueeze(2).broadcast_to([1, OVER, E]), ALU.is_le))
                ch.link(V.reduce_sum(bef[:, E:NB], bcmp[:], AX_X))
                ch.link(V.tensor_scalar(bef[:, E:NB], bef[:, E:NB], float(E - 1), None, ALU.min))
                ch.mark(V.tensor_copy(rt.block_e[:], bef[:]))
                ch.mark(V.tensor_copy(rt.used[:], cnt[0:1, 2, E - 1:E]))
                dve.wait_ge(toks_done, 1)
                ch.mark(V.tensor_copy(rt.row_tok[:], ps_t[:, 0:NB]))
                ch.settle()


def experts(core, name, rt, xn_rows, scale, shift, w_gate, w_up, w_down, y_rows):
    nc = core.nc
    F = w_gate.shape[2]
    KF = F // P
    E = rt.E
    assert E % 2 == 0
    gate_v = w_gate.rearrange("e (k p) n -> e p k n", p=P)
    up_v = w_up.rearrange("e (k p) n -> e p k n", p=P)
    down_v = w_down.rearrange("e (k p) n -> e p k n", p=P)
    x_loaded = [core.sem(f"{name}_x_loaded{b}") for b in range(2)]
    gu_loaded = [core.sem(f"{name}_gu_loaded{b}") for b in range(2)]
    d_loaded = [core.sem(f"{name}_d_loaded{b}") for b in range(2)]
    rows_named = core.sem(f"{name}_rows_named")
    rows_seen = core.sem(f"{name}_rows_seen")
    x_turned = core.sem(f"{name}_x_turned")
    xT_ready = [core.sem(f"{name}_xT_ready_act"), core.sem(f"{name}_xT_ready_dve")]
    gu_done = core.sem(f"{name}_gu_done")
    silu_done = core.sem(f"{name}_silu_done")
    h_ready = core.sem(f"{name}_h_ready")
    h_turned = core.sem(f"{name}_h_turned")
    hT_ready = core.sem(f"{name}_hT_ready")
    y_done = core.sem(f"{name}_y_done")
    y_copied = [core.sem(f"{name}_y_copied_act"), core.sem(f"{name}_y_copied_dve")]
    stored = [core.sem(f"{name}_stored{b}") for b in range(2)]
    with ExitStack() as ctx:
        sb = lambda n, s, d=F32: ctx.enter_context(nc.sbuf_tensor(f"{name}_{n}", s, d))
        gu = sb("gu", [P, 2, KD, 2, F])
        dn = sb("dn", [P, 2, KF, D])
        rows = [sb(f"rows{b}", [P, 1], I32) for b in range(2)]
        x = [sb(f"x{b}", [P, D]) for b in range(2)]
        xT = sb("xT", [P, 2, KD, P])
        sg = sb("sg", [P, F])
        h = sb("h", [P, 2, F])
        hT = sb("hT", [P, KF, P])
        y = sb("y", [P, 2, D])
        ps_x = ctx.enter_context(nc.psum_tensor(f"{name}_ps_x", [P, 2 * BANK], F32))
        ps_g = ctx.enter_context(nc.psum_tensor(f"{name}_ps_g", [P, 2, BANK], F32))
        ps_h = ctx.enter_context(nc.psum_tensor(f"{name}_ps_h", [P, BANK], F32))
        ps_y = ctx.enter_context(nc.psum_tensor(f"{name}_ps_y", [P, 2 * BANK], F32))
        up_bank = 1 if F == BANK else 0
        up_at = 0 if F == BANK else F

        with nc.Block() as block:

            @block.sync
            def _(sp):
                def load(half, par):
                    n = half * 2 + par
                    sp.wait_ge(gu_done, n + 1)
                    sp.dma_start(gu[:, par, :, 0, :], gate_v[bass.ds(n, 1)].rearrange("e p k n -> p (e k) n")) \
                        .then_inc(gu_loaded[par], 16)
                    sp.dma_start(gu[:, par, :, 1, :], up_v[bass.ds(n, 1)].rearrange("e p k n -> p (e k) n")) \
                        .then_inc(gu_loaded[par], 16)
                    sp.wait_ge(y_done, n * 2 + 2)
                    sp.dma_start(dn[:, par], down_v[bass.ds(n, 1)].rearrange("e p k n -> p (e k) n")) \
                        .then_inc(d_loaded[par], 16)

                with sp.Fori(0, E // 2) as it:
                    for par in range(2):
                        load(it, par)

            @block.gpsimd
            def _(pool):
                def gather(half, par):
                    n = half * 2 + par
                    pool.wait_ge(x_turned, n + 1)
                    nc.gpsimd.tensor_copy(rows[par][:], rt.row_tok[:, bass.ds(n, 1)]).then_inc(rows_named, 1)
                    pool.wait_ge(rows_named, n + 1)
                    pool.sem_inc(rows_seen, 1)
                    pool.indirect_dma_start(out=x[par][:], out_offset=None, in_=xn_rows,
                                            in_offset=bass.IndirectOffsetOnAxis(ap=rows[par][:, 0:1], axis=0)) \
                        .then_inc(x_loaded[par], 16)

                gather(0, 0)
                gather(0, 1)
                with pool.Fori(0, E // 2 - 1) as it:
                    gather(it + 1, 0)
                    gather(it + 1, 1)

            @block.tensor
            def _(pe):
                pe.sem_inc(x_turned, 2)
                pe.sem_inc(gu_done, 2)
                pe.sem_inc(y_done, 4)
                pe.sem_inc(h_turned, 1)

                def turn_x(half, par):
                    pe.wait_ge(x_loaded[par], half * 16 + 16)
                    for z in range(2):
                        pe.wait_ge(xT_ready[z], half * 2 + (par + 1))
                    for k in range(KD):
                        last = nc.tensor.transpose(ps_x[:, k * P:(k + 1) * P], x[par][:, k * P:(k + 1) * P], core.ident[:])
                    last.then_inc(x_turned, 1)

                def gate_up(half, par):
                    for z in range(2):
                        pe.wait_ge(xT_ready[z], half * 2 + (par + 2))
                    pe.wait_ge(gu_loaded[par], half * 32 + 32)
                    pe.wait_ge(h_ready, half * 2 + (par + 1))
                    for k in range(KD):
                        if F == BANK:
                            for z in range(2):
                                last = nc.tensor.matmul(ps_g[:, z], xT[:, par, k, :], gu[:, par, k, z, :],
                                                        start=(k == 0), stop=(k == KD - 1))
                        else:
                            last = nc.tensor.matmul(ps_g[:, 0], xT[:, par, k, :],
                                                    gu[:, par, k].rearrange("p z n -> p (z n)"),
                                                    start=(k == 0), stop=(k == KD - 1))
                    last.then_inc(gu_done, 1)

                def turn_h(half, par):
                    pe.wait_ge(h_ready, half * 2 + (par + 2))
                    pe.wait_ge(hT_ready, half * 2 + (par + 1))
                    for k in range(KF):
                        last = nc.tensor.transpose(ps_h[:, k * P:(k + 1) * P], h[:, par, k * P:(k + 1) * P], core.ident[:])
                    last.then_inc(h_turned, 1)

                def down(half, par):
                    pe.wait_ge(hT_ready, half * 2 + (par + 2))
                    pe.wait_ge(d_loaded[par], half * 16 + 16)
                    for z in range(2):
                        pe.wait_ge(y_copied[z], half * 2 + (par + 1))
                        for k in range(KF):
                            last = nc.tensor.matmul(ps_y[:, z * BANK:(z + 1) * BANK], hT[:, k, :],
                                                    dn[:, par, k, z * BANK:(z + 1) * BANK],
                                                    start=(k == 0), stop=(k == KF - 1))
                        last.then_inc(y_done, 1)

                turn_x(0, 0)
                gate_up(0, 0)
                turn_x(0, 1)
                turn_h(0, 0)
                with pe.Fori(0, E // 2 - 1) as it:
                    gate_up(it, 1)
                    down(it, 0)
                    turn_x(it + 1, 0)
                    turn_h(it, 1)
                    gate_up(it + 1, 0)
                    down(it, 1)
                    turn_x(it + 1, 1)
                    turn_h(it + 1, 0)
                last_half = E // 2 - 1
                gate_up(last_half, 1)
                down(last_half, 0)
                turn_h(last_half, 1)
                down(last_half, 1)

            @block.scalar
            def _(act):
                def scale_x(half, par):
                    n = half * 2 + par
                    act.wait_ge(x_turned, n + 3)
                    act.wait_ge(gu_done, n + 1)
                    for k in range(KD // 2):
                        last = nc.scalar.activation(xT[:, par, k, :], ps_x[:, k * P:(k + 1) * P], ACT.Identity,
                                                    scale=scale[:, k:k + 1],
                                                    bias=0.0 if shift is None else shift[:, k:k + 1])
                    last.then_inc(xT_ready[0], 1)

                def silu(half, par):
                    n = half * 2 + par
                    act.wait_ge(gu_done, n + 3)
                    act.wait_ge(h_ready, n + 1)
                    nc.scalar.activation(sg[:], ps_g[:, 0, 0:F], ACT.Silu).then_inc(silu_done, 1)

                def copy_y(half, par):
                    n = half * 2 + par
                    act.wait_ge(y_done, n * 2 + 5)
                    act.wait_ge(stored[par], half * 16 + 16)
                    nc.scalar.copy(y[:, par, 0:BANK], ps_y[:, 0:BANK]).then_inc(y_copied[0], 1)

                def store(half, par):
                    n = half * 2 + par
                    for z in range(2):
                        act.wait_ge(y_copied[z], n + 2)
                    act.dma_start(y_rows[bass.ds(n * SLOTS, SLOTS), :], y[:, par]).then_inc(stored[par], 16)

                act.sem_inc(xT_ready[0], 1)
                act.sem_inc(y_copied[0], 1)
                for b in range(2):
                    act.sem_inc(stored[b], 16)
                scale_x(0, 0)
                silu(0, 0)
                scale_x(0, 1)
                with act.Fori(0, E // 2 - 1) as it:
                    silu(it, 1)
                    copy_y(it, 0)
                    scale_x(it + 1, 0)
                    store(it, 0)
                    silu(it + 1, 0)
                    copy_y(it, 1)
                    scale_x(it + 1, 1)
                    store(it, 1)
                last_half = E // 2 - 1
                silu(last_half, 1)
                copy_y(last_half, 0)
                store(last_half, 0)
                copy_y(last_half, 1)
                store(last_half, 1)
                for b in range(2):
                    act.wait_ge(stored[b], 16 * (E // 2 + 1))

            @block.vector
            def _(dve):
                def scale_x(half, par):
                    n = half * 2 + par
                    dve.wait_ge(x_turned, n + 3)
                    dve.wait_ge(gu_done, n + 1)
                    for k in range(KD // 2, KD):
                        args = (ALU.mult,) if shift is None else (ALU.mult, ALU.add)
                        last = nc.vector.tensor_scalar(xT[:, par, k, :], ps_x[:, k * P:(k + 1) * P], scale[:, k:k + 1],
                                                       None if shift is None else shift[:, k:k + 1], *args)
                    last.then_inc(xT_ready[1], 1)

                def hidden(half, par):
                    n = half * 2 + par
                    dve.wait_ge(silu_done, n + 1)
                    dve.wait_ge(h_turned, n + 1)
                    nc.vector.tensor_tensor(h[:, par], sg[:], ps_g[:, up_bank, up_at:up_at + F], ALU.mult) \
                        .then_inc(h_ready, 1)

                def copy_h(half, par):
                    n = half * 2 + par
                    dve.wait_ge(h_turned, n + 2)
                    dve.wait_ge(y_done, n * 2 + 4)
                    nc.vector.tensor_copy(hT[:].rearrange("p k t -> p (k t)"), ps_h[:, 0:KF * P]).then_inc(hT_ready, 1)

                def copy_y(half, par):
                    n = half * 2 + par
                    dve.wait_ge(y_done, n * 2 + 6)
                    dve.wait_ge(stored[par], half * 16 + 16)
                    nc.vector.tensor_copy(y[:, par, BANK:], ps_y[:, BANK:]).then_inc(y_copied[1], 1)

                for counter in (xT_ready[1], y_copied[1], h_ready, hT_ready):
                    dve.sem_inc(counter, 1)
                scale_x(0, 0)
                hidden(0, 0)
                scale_x(0, 1)
                copy_h(0, 0)
                with dve.Fori(0, E // 2 - 1) as it:
                    hidden(it, 1)
                    copy_y(it, 0)
                    scale_x(it + 1, 0)
                    copy_h(it, 1)
                    hidden(it + 1, 0)
                    copy_y(it, 1)
                    scale_x(it + 1, 1)
                    copy_h(it + 1, 0)
                last_half = E // 2 - 1
                hidden(last_half, 1)
                copy_y(last_half, 0)
                copy_h(last_half, 1)
                copy_y(last_half, 1)


def experts_beyond(core, name, rt, xn_rows, scale, shift, w_gate, w_up, w_down, y_rows):
    nc = core.nc
    F = w_gate.shape[2]
    KF = F // P
    E = rt.E
    gate_v = w_gate.rearrange("e (k p) n -> e p k n", p=P)
    up_v = w_up.rearrange("e (k p) n -> e p k n", p=P)
    down_v = w_down.rearrange("e (k p) n -> e p k n", p=P)
    x_loaded = core.sem(f"{name}_x_loaded")
    w_loaded = core.sem(f"{name}_w_loaded")
    rows_named = core.sem(f"{name}_rows_named")
    rows_seen = core.sem(f"{name}_rows_seen")
    x_turned = core.sem(f"{name}_x_turned")
    xT_ready = [core.sem(f"{name}_xT_ready_act"), core.sem(f"{name}_xT_ready_dve")]
    gu_done = core.sem(f"{name}_gu_done")
    silu_done = core.sem(f"{name}_silu_done")
    h_ready = core.sem(f"{name}_h_ready")
    h_turned = core.sem(f"{name}_h_turned")
    hT_ready = core.sem(f"{name}_hT_ready")
    y_done = core.sem(f"{name}_y_done")
    y_copied = [core.sem(f"{name}_y_copied_act"), core.sem(f"{name}_y_copied_dve")]
    stored = core.sem(f"{name}_stored")
    store_seen = core.sem(f"{name}_store_seen")
    with ExitStack() as ctx:
        sb = lambda n, s, d=F32: ctx.enter_context(nc.sbuf_tensor(f"{name}_{n}", s, d))
        gu, dn = sb("gu", [P, KD, 2, F]), sb("dn", [P, KF, D])
        rows, x, xT = sb("rows", [P, 1], I32), sb("x", [P, D]), sb("xT", [P, KD, P])
        sg, h, hT, y = sb("sg", [P, F]), sb("h", [P, F]), sb("hT", [P, KF, P]), sb("y", [P, D])
        ps_x = ctx.enter_context(nc.psum_tensor(f"{name}_ps_x", [P, 2 * BANK], F32))
        ps_g = ctx.enter_context(nc.psum_tensor(f"{name}_ps_g", [P, 2, BANK], F32))
        ps_h = ctx.enter_context(nc.psum_tensor(f"{name}_ps_h", [P, BANK], F32))
        ps_y = ctx.enter_context(nc.psum_tensor(f"{name}_ps_y", [P, 2 * BANK], F32))
        with nc.Block() as block:

            def each_in_use(eng, body):
                used = eng.value_load(rt.used[0:1, 0:1], min_val=0, max_val=OVER)
                with eng.Fori(0, OVER) as j:
                    with eng.If(j < used):
                        body(j)

            @block.sync
            def _(sp):
                def load(j):
                    sp.wait_ge(stored, j * 16 + 16)
                    e = sp.value_load(rt.block_e[0:1, bass.ds(j + E, 1)], min_val=0, max_val=E - 1)
                    for dst, src in ((gu[:, :, 0, :], gate_v), (gu[:, :, 1, :], up_v), (dn[:], down_v)):
                        sp.dma_start(dst, src[bass.ds(e, 1)].rearrange("e p k n -> p (e k) n")).then_inc(w_loaded, 16)

                each_in_use(sp, load)

            @block.gpsimd
            def _(pool):
                def gather(j):
                    pool.wait_ge(stored, j * 16 + 16)
                    nc.gpsimd.tensor_copy(rows[:], rt.row_tok[:, bass.ds(j + E, 1)]).then_inc(rows_named, 1)
                    pool.wait_ge(rows_named, j + 1)
                    pool.sem_inc(rows_seen, 1)
                    pool.indirect_dma_start(out=x[:], out_offset=None, in_=xn_rows,
                                            in_offset=bass.IndirectOffsetOnAxis(ap=rows[:, 0:1], axis=0)) \
                        .then_inc(x_loaded, 16)

                each_in_use(pool, gather)

            @block.tensor
            def _(pe):
                def products(j):
                    pe.wait_ge(x_loaded, j * 16 + 16)
                    for k in range(KD):
                        last = nc.tensor.transpose(ps_x[:, k * P:(k + 1) * P], x[:, k * P:(k + 1) * P], core.ident[:])
                    last.then_inc(x_turned, 1)
                    for z in range(2):
                        pe.wait_ge(xT_ready[z], j + 1)
                    pe.wait_ge(w_loaded, j * 48 + 48)
                    for z in range(2):
                        for k in range(KD):
                            last = nc.tensor.matmul(ps_g[:, z, 0:F], xT[:, k, :], gu[:, k, z, :],
                                                    start=(k == 0), stop=(k == KD - 1))
                    last.then_inc(gu_done, 1)
                    pe.wait_ge(h_ready, j + 1)
                    for k in range(KF):
                        last = nc.tensor.transpose(ps_h[:, k * P:(k + 1) * P], h[:, k * P:(k + 1) * P], core.ident[:])
                    last.then_inc(h_turned, 1)
                    pe.wait_ge(hT_ready, j + 1)
                    for z in range(2):
                        for k in range(KF):
                            last = nc.tensor.matmul(ps_y[:, z * BANK:(z + 1) * BANK], hT[:, k, :],
                                                    dn[:, k, z * BANK:(z + 1) * BANK], start=(k == 0), stop=(k == KF - 1))
                    last.then_inc(y_done, 1)

                each_in_use(pe, products)

            @block.scalar
            def _(act):
                act.sem_inc(stored, 16)

                def half(j):
                    act.wait_ge(x_turned, j + 1)
                    for k in range(KD // 2):
                        last = nc.scalar.activation(xT[:, k, :], ps_x[:, k * P:(k + 1) * P], ACT.Identity,
                                                    scale=scale[:, k:k + 1],
                                                    bias=0.0 if shift is None else shift[:, k:k + 1])
                    last.then_inc(xT_ready[0], 1)
                    act.wait_ge(gu_done, j + 1)
                    nc.scalar.activation(sg[:], ps_g[:, 0, 0:F], ACT.Silu).then_inc(silu_done, 1)
                    act.wait_ge(y_done, j + 1)
                    nc.scalar.copy(y[:, 0:BANK], ps_y[:, 0:BANK]).then_inc(y_copied[0], 1)
                    for z in range(2):
                        act.wait_ge(y_copied[z], j + 1)
                    act.dma_start(y_rows[bass.ds((j + E) * SLOTS, SLOTS), :], y[:]).then_inc(stored, 16)
                    act.wait_ge(stored, j * 16 + 32)
                    act.sem_inc(store_seen, 1)

                each_in_use(act, half)

            @block.vector
            def _(dve):
                def half(j):
                    dve.wait_ge(x_turned, j + 1)
                    for k in range(KD // 2, KD):
                        args = (ALU.mult,) if shift is None else (ALU.mult, ALU.add)
                        last = nc.vector.tensor_scalar(xT[:, k, :], ps_x[:, k * P:(k + 1) * P], scale[:, k:k + 1],
                                                       None if shift is None else shift[:, k:k + 1], *args)
                    last.then_inc(xT_ready[1], 1)
                    dve.wait_ge(silu_done, j + 1)
                    nc.vector.tensor_tensor(h[:], sg[:], ps_g[:, 1, 0:F], ALU.mult).then_inc(h_ready, 1)
                    dve.wait_ge(h_turned, j + 1)
                    nc.vector.tensor_copy(hT[:].rearrange("p k t -> p (k t)"), ps_h[:, 0:KF * P]).then_inc(hT_ready, 1)
                    dve.wait_ge(y_done, j + 1)
                    nc.vector.tensor_copy(y[:, BANK:], ps_y[:, BANK:]).then_inc(y_copied[1], 1)

                each_in_use(dve, half)


def combine(core, name, rt, y_rows, x, gate, out):
    nc = core.nc
    y_in = [core.sem(f"{name}_y_in{b}") for b in range(2)]
    x_in = [core.sem(f"{name}_x_in{b}") for b in range(2)]
    dest_ready = core.sem(f"{name}_dest_ready")
    weighted = core.sem(f"{name}_weighted")
    own = core.sem(f"{name}_dve")
    added = core.sem(f"{name}_added")
    stored = [core.sem(f"{name}_stored{b}") for b in range(2)]
    with ExitStack() as ctx:
        sb = lambda n, s, d=F32: ctx.enter_context(nc.sbuf_tensor(f"{name}_{n}", s, d))
        y = [[sb(f"y{b}{z}", [P, D]) for z in range(2)] for b in range(2)]
        xt = sb("x", [P, 2, D])
        r = sb("r", [P, 2, D])
        with nc.Block() as block:

            @block.gpsimd
            def _(pool):
                for i in range(TT):
                    if i >= 2:
                        pool.wait_ge(added, i - 1)
                    for z in range(2):
                        pool.indirect_dma_start(out=y[i % 2][z][:], out_offset=None, in_=y_rows,
                                                in_offset=bass.IndirectOffsetOnAxis(ap=rt.dest[:, i, z:z + 1], axis=0)) \
                            .then_inc(y_in[i % 2], 16)

            @block.sync
            def _(sp):
                for i in range(TT + 1):
                    if i < TT:
                        if i >= 2:
                            sp.wait_ge(added, i - 1)
                        sp.dma_start(xt[:, i % 2], x[i * P:(i + 1) * P, :]).then_inc(x_in[i % 2], 16)
                    if i >= 1:
                        sp.wait_ge(added, i)
                        sp.dma_start(out[(i - 1) * P:i * P, :], r[:, (i - 1) % 2]).then_inc(stored[(i - 1) % 2], 16)
                for b in range(2):
                    sp.wait_ge(stored[b], 16 * TT // 2)

            @block.scalar
            def _(act):
                for i in range(TT):
                    act.wait_ge(y_in[i % 2], 32 * (i // 2 + 1))
                    if i >= 2:
                        act.wait_ge(stored[i % 2], 16 * (i // 2))
                    nc.scalar.activation(r[:, i % 2], y[i % 2][0][:], ACT.Copy, scale=rt.weight[:, i, 0:1]) \
                        .then_inc(weighted, 1)

            @block.vector
            def _(dve):
                ch = Chain(dve, own)
                for i in range(TT):
                    dve.wait_ge(weighted, i + 1)
                    rr = r[:, i % 2]
                    ch.link(nc.vector.scalar_tensor_tensor(rr, y[i % 2][1][:], rt.weight[:, i, 1:2], rr, ALU.mult, ALU.add))
                    if gate is not None:
                        ch.link(nc.vector.tensor_tensor(rr, rr, gate, ALU.mult))
                    dve.wait_ge(x_in[i % 2], 16 * (i // 2 + 1))
                    nc.vector.tensor_tensor(rr, rr, xt[:, i % 2], ALU.add).then_inc(added, 1)


def ffn1(core, inp, mix, x1, xn, y, x2):
    nc = core.nc
    with ExitStack() as ctx:
        mixT = pair(core, ctx, "mixT", [P, KD, T])
        turn_rows(core, "mixturn", mix, mixT, KD)
        residual_product(core, "outproj", mixT, inp["w_out"][0], inp["x"][0], core.gate_rows[:, 0], x1)
    with ExitStack() as ctx:
        core.ctx_keep = lambda n, s, d: ctx.enter_context(nc.sbuf_tensor(n, s, d))
        rt = Routing(core, "rt1", inp["expert_w_gate"].shape[1])
        shift = core.mods[:, 0, 3 * KD:4 * KD]
        with ExitStack() as c2:
            h2T = c2.enter_context(nc.sbuf_tensor("h2T", [P, KD, T], F32))
            tiles = [(x1[i * P:(i + 1) * P, :], core.ffn_scale[:], shift) for i in range(TT)]
            norm_transpose(core, "norm2", tiles, h2T, xn)
            route(core, "route1", h2T, inp["router_group_w"][0], inp["router_expert_w"][0],
                  inp["router_group_b"][0], inp["router_expert_b"][0], rt, y)
        experts(core, "exp1", rt, xn, core.ffn_scale, shift, inp["expert_w_gate"][0], inp["expert_w_up"][0],
                inp["expert_w_down"][0], y)
        experts_beyond(core, "over1", rt, xn, core.ffn_scale, shift, inp["expert_w_gate"][0],
                       inp["expert_w_up"][0], inp["expert_w_down"][0], y)
        combine(core, "comb1", rt, y, x1, core.gate_rows[:, 1], x2)


def row_norm(core, name, x, gain, out):
    nc = core.nc
    x_in = [core.sem(f"{name}_x_in{b}") for b in range(2)]
    g_in = core.sem(f"{name}_g_in")
    own = core.sem(f"{name}_dve")
    summed = core.sem(f"{name}_summed")
    rooted = core.sem(f"{name}_rooted")
    ready = core.sem(f"{name}_ready")
    stored = [core.sem(f"{name}_stored{b}") for b in range(2)]
    with ExitStack() as ctx:
        sb = lambda n, s, d=F32: ctx.enter_context(nc.sbuf_tensor(f"{name}_{n}", s, d))
        xt, sq, r = sb("x", [P, 2, D]), sb("sq", [P, 2, D]), sb("r", [P, 2, D])
        g = sb("g", [P, D])
        st = sb("st", [P, TT, 3])
        with nc.Block() as block:

            @block.sync
            def _(sp):
                sp.dma_start(g[:], gain.partition_broadcast(P)).then_inc(g_in, 16)
                for i in range(TT):
                    if i >= 2:
                        sp.wait_ge(ready, i - 1)
                    sp.dma_start(xt[:, i % 2], x[i * P:(i + 1) * P, :]).then_inc(x_in[i % 2], 16)

            @block.scalar
            def _(act):
                for i in range(TT):
                    act.wait_ge(x_in[i % 2], 16 * (i // 2 + 1))
                    if i >= 2:
                        act.wait_ge(summed, i - 1)
                    nc.scalar.activation(sq[:, i % 2], xt[:, i % 2], ACT.Square, accum_out=st[:, i, 0:1]) \
                        .then_inc(summed, 1)
                    act.wait_ge(summed, i + 1)
                    nc.scalar.activation(st[:, i, 1:2], st[:, i, 0:1], ACT.Sqrt, scale=1.0 / D,
                                         bias=core.eps[:]).then_inc(rooted, 1)

            @block.vector
            def _(dve):
                ch = Chain(dve, own)
                dve.wait_ge(g_in, 16)
                for i in range(TT):
                    dve.wait_ge(rooted, i + 1)
                    if i >= 2:
                        dve.wait_ge(stored[i % 2], 16 * (i // 2))
                    ch.link(nc.vector.reciprocal(st[:, i, 2:3], st[:, i, 1:2]))
                    nc.vector.scalar_tensor_tensor(r[:, i % 2], xt[:, i % 2], st[:, i, 2:3], g[:], ALU.mult, ALU.mult) \
                        .then_inc(ready, 1)

            @block.gpsimd
            def _(pool):
                for i in range(TT):
                    pool.wait_ge(ready, i + 1)
                    pool.dma_start(out[i * P:(i + 1) * P, :], r[:, i % 2]).then_inc(stored[i % 2], 16)
                for b in range(2):
                    pool.wait_ge(stored[b], 16 * TT // 2)


CONV = 4
LRU_C = 8.0


def recurrent_branch(core, inp, projT, hg):
    nc = core.nc
    v, at = core.v2, core.at2
    x_in = [core.sem(f"rnn_x_in{b}") for b in range(2)]
    w_in = core.sem("rnn_w_in")
    y_in = core.sem("rnn_y_in")
    padded = core.sem("rnn_padded")
    own = core.sem("rnn_dve")
    acts = core.sem("rnn_act")
    conv_done = core.sem("rnn_conv_done")
    gates_done = core.sem("rnn_gates_done")
    sig_done = core.sem("rnn_sig_done")
    lam_exp = core.sem("rnn_lam_exp")
    lam_ready = core.sem("rnn_lam_ready")
    decay_done = core.sem("rnn_decay_done")
    square_ready = core.sem("rnn_square_ready")
    root_done = core.sem("rnn_root_done")
    gelu_done = core.sem("rnn_gelu_done")
    with ExitStack() as ctx:
        sb = lambda n, s, d=F32: ctx.enter_context(nc.sbuf_tensor("rnn_" + n, s, d))
        xp = [sb(f"xp{b}", [P, CONV - 1 + T]) for b in range(2)]
        xc = sb("xc", [P, KD, T])
        rg = sb("rg", [P, KD, T])
        ig = sb("ig", [P, KD, T])
        de = sb("de", [P, KD, T])
        wa, wx = sb("wa", [P, KD, P]), sb("wx", [P, KD, P])
        q = sb("q", [P, 2, T])
        lam = sb("lam", [P, 8, KD])
        ps = ctx.enter_context(nc.psum_tensor("rnn_ps", [P, 2, 2, 2 * BANK], F32))
        gy = hg
        with nc.Block() as block:

            @block.sync
            def _(sp):
                sp.dma_start(wa[:], inp["lru_wa_2"][0].rearrange("n k j -> k n j")).then_inc(w_in, 16)
                sp.dma_start(wx[:], inp["lru_wx_2"][0].rearrange("n k j -> k n j")).then_inc(w_in, 16)
                sp.wait_ge(padded, 1)
                for c in range(KD):
                    if c >= 2:
                        sp.wait_ge(conv_done, c - 1)
                    sp.dma_start(xp[c % 2][:, CONV - 1:], projT[c * P:(c + 1) * P, :]).then_inc(x_in[c % 2], 16)
                sp.dma_start(gy[:], projT[D:2 * D, :].rearrange("(k p) t -> p k t", p=P)).then_inc(y_in, 16)

            @block.gpsimd
            def _(pool):
                for b in range(2):
                    last = nc.gpsimd.memset(xp[b][:, 0:CONV - 1], 0.0)
                last.then_inc(padded, 1)

            @block.tensor
            def _(pe):
                pe.wait_ge(w_in, 32)
                for c in range(KD):
                    pe.wait_ge(conv_done, c + 1)
                    if c >= 2:
                        pe.wait_ge(sig_done, 2 * (c - 1))
                    for g, w in enumerate((wa, wx)):
                        for h in range(2):
                            last = nc.tensor.matmul(ps[:, c % 2, g, h * BANK:(h + 1) * BANK], w[:, c, :],
                                                    xc[:, c, h * BANK:(h + 1) * BANK], start=True, stop=True)
                    last.then_inc(gates_done, 1)

            @block.scalar
            def _(act):
                nc.scalar.activation(lam[:, 0], v[:, at["lru_lambda"]], ACT.Abs).then_inc(acts, 1)
                act.wait_ge(acts, 1)
                nc.scalar.activation(lam[:, 1], lam[:, 0], ACT.Exp, scale=-1.0).then_inc(lam_exp, 1)
                for c in range(KD):
                    act.wait_ge(gates_done, c + 1)
                    for g, (dst, b) in enumerate(((rg, "lru_ba"), (ig, "lru_bx"))):
                        col = at[b].start + c
                        nc.scalar.activation(dst[:, c], ps[:, c % 2, g], ACT.Sigmoid, bias=v[:, col:col + 1]) \
                            .then_inc(sig_done, 1)
                act.wait_ge(lam_ready, 1)
                act.wait_ge(sig_done, 2 * KD)
                for c in range(KD):
                    nc.scalar.activation(de[:, c], rg[:, c], ACT.Exp, scale=lam[:, 6, c:c + 1]).then_inc(decay_done, 1)
                    act.wait_ge(decay_done, 2 * c + 1)
                    nc.scalar.activation(rg[:, c], rg[:, c], ACT.Tanh, scale=lam[:, 7, c:c + 1]).then_inc(decay_done, 1)
                for c in range(KD):
                    act.wait_ge(square_ready, c + 1)
                    nc.scalar.activation(rg[:, c], rg[:, c], ACT.Sqrt).then_inc(root_done, 1)
                act.wait_ge(y_in, 16)
                for c in range(KD):
                    nc.scalar.activation(gy[:, c], gy[:, c], ACT.Gelu_apprx_tanh).then_inc(gelu_done, 1)

            @block.vector
            def _(dve):
                ch = Chain(dve, own)
                V = nc.vector
                dve.wait_ge(lam_exp, 1)
                ch.link(V.tensor_scalar(lam[:, 2], lam[:, 1], 2.0, None, ALU.add))
                ch.link(V.reciprocal(lam[:, 3], lam[:, 2]))
                ch.link(V.tensor_tensor(lam[:, 2], lam[:, 1], lam[:, 3], ALU.mult))
                ch.link(V.tensor_tensor(lam[:, 3], lam[:, 2], lam[:, 2], ALU.mult))
                ch.link(V.tensor_scalar(lam[:, 4], lam[:, 3], 1.0 / 17, 1.0 / 15, ALU.mult, ALU.add))
                for odd in (13, 11, 9, 7, 5, 3, 1):
                    ch.link(V.tensor_tensor(lam[:, 4], lam[:, 4], lam[:, 3], ALU.mult))
                    ch.link(V.tensor_scalar(lam[:, 4], lam[:, 4], 1.0 / odd, None, ALU.add))
                ch.link(V.tensor_tensor(lam[:, 4], lam[:, 4], lam[:, 2], ALU.mult))
                ch.link(V.tensor_scalar(lam[:, 5], v[:, at["lru_lambda"]], -1.0, 0.0, ALU.mult, ALU.max))
                ch.link(V.scalar_tensor_tensor(lam[:, 5], lam[:, 4], 2.0, lam[:, 5], ALU.mult, ALU.add))
                V.tensor_scalar(lam[:, 6], lam[:, 5], -LRU_C, None, ALU.mult)
                V.tensor_scalar(lam[:, 7], lam[:, 5], LRU_C, None, ALU.mult).then_inc(lam_ready, 1)
                for c in range(KD):
                    dve.wait_ge(x_in[c % 2], 16 * (c // 2 + 1))
                    tap = lambda j: v[:, at["conv_w"].start + j * KD + c:at["conv_w"].start + j * KD + c + 1]
                    bias = v[:, at["conv_b"].start + c:at["conv_b"].start + c + 1]
                    ch.link(V.tensor_scalar(xc[:, c], xp[c % 2][:, 0:T], tap(0), bias, ALU.mult, ALU.add))
                    for j in range(1, CONV):
                        ins = V.scalar_tensor_tensor(xc[:, c], xp[c % 2][:, j:j + T], tap(j), xc[:, c], ALU.mult, ALU.add)
                        if j < CONV - 1:
                            ch.link(ins)
                    ins.then_inc(conv_done, 1)
                for c in range(KD):
                    dve.wait_ge(decay_done, 2 * c + 2)
                    ch.link(V.tensor_tensor(q[:, c % 2], de[:, c], de[:, c], ALU.mult))
                    V.scalar_tensor_tensor(rg[:, c], q[:, c % 2], 1.0, rg[:, c], ALU.add, ALU.mult).then_inc(square_ready, 1)
                    dve.wait_ge(conv_done, c + 1)
                    ch.mark(V.tensor_tensor(ig[:, c], xc[:, c], ig[:, c], ALU.mult))
                ch.settle()
                for c in range(KD):
                    dve.wait_ge(root_done, c + 1)
                    ch.link(V.tensor_tensor(ig[:, c], ig[:, c], rg[:, c], ALU.mult))
                    ch.link(V.tensor_tensor_scan(xc[:, c], de[:, c], ig[:, c], 0.0, ALU.mult, ALU.add))
                    dve.wait_ge(gelu_done, c + 1)
                    ch.mark(V.tensor_tensor(hg[:, c], xc[:, c], gy[:, c], ALU.mult))
                ch.settle()


MLA_H, NOPE, ROPE, MLA_V = 8, 128, 64, 128
QK = NOPE + ROPE


def mla_heads(core, inp, q_rows, kv_rows, pe_cols, qnT, knT, qrT, krT):
    nc = core.nc
    TWO_PI = 2 * np.pi
    C1 = 6.28125
    C2 = float(np.float32(np.float32((TWO_PI - C1) * 2 ** 20).astype(np.int32)) / 2 ** 20)
    C3 = TWO_PI - C1 - C2
    MAGIC = 12582912.0
    PI_DOWN = 3.1415925
    small_in = core.sem("mh_small_in")
    x_in = [core.sem(f"mh_x_in{b}") for b in range(2)]
    own = core.sem("mh_dve")
    pools = core.sem("mh_pool")
    ang_ready = core.sem("mh_ang_ready")
    sin_done = core.sem("mh_sin_done")
    sq_done = core.sem("mh_sq_done")
    sums_ready = core.sem("mh_sums_ready")
    rooted = core.sem("mh_rooted")
    nope_ready = core.sem("mh_nope_ready")
    rope_ready = core.sem("mh_rope_ready")
    turned = core.sem("mh_turned")
    copied = core.sem("mh_copied")
    H = MLA_H
    with ExitStack() as ctx:
        sb = lambda n, s, d=F32: ctx.enter_context(nc.sbuf_tensor("mh_" + n, s, d))
        posi = sb("posi", [P, TT], I32)
        pos = sb("pos", [P, TT])
        inv = sb("inv", [P, ROPE // 2])
        ang = sb("ang", [P, 2, TT, ROPE // 2])
        tmp = sb("tmp", [P, TT, ROPE // 2])
        gq, gk = sb("gq", [P, QK]), sb("gk", [P, QK])
        q = sb("q", [P, 2, H, QK])
        kn = sb("kn", [P, 2, H, NOPE])
        pe_in = sb("pe_in", [P, 2, ROPE])
        sq = sb("sq", [P, H, QK + NOPE])
        sp_ = sb("sp", [P, ROPE])
        st = sb("st", [P, TT, 4, 2 * H])
        qk = sb("qk", [P, 2 * H, QK])
        ro = sb("ro", [P, 2 * H, ROPE])
        t1 = sb("t1", [P, 2 * H, ROPE])
        ps = ctx.enter_context(nc.psum_tensor("mh_ps", [P, 8, BANK], F32))
        with nc.Block() as block:

            @block.sync
            def _(sp):
                sp.dma_start(posi[:], inp["positions_2"][0].rearrange("(t p) -> p t", p=P),
                             allow_slow_non_contiguous=True).then_inc(small_in, 16)
                sp.dma_start(inv[:], inp["inv_freq"].partition_broadcast(P)).then_inc(small_in, 16)
                sp.dma_start(gq[:], inp["qk_norm_q_g_2"][0].partition_broadcast(P)).then_inc(small_in, 16)
                sp.dma_start(gk[:], inp["qk_norm_k_g_2"][0].partition_broadcast(P)).then_inc(small_in, 16)
                for i in range(TT):
                    b = i % 2
                    if i >= 2:
                        sp.wait_ge(nope_ready, i - 1)
                    r = slice(i * P, (i + 1) * P)
                    sp.dma_start(q[:, b], q_rows[r, :].rearrange("p (h d) -> p h d", h=H)).then_inc(x_in[b], 16)
                    sp.dma_start(kn[:, b], kv_rows[r, :].rearrange("p (h d) -> p h d", h=H)[:, :, 0:NOPE]) \
                        .then_inc(x_in[b], 16)
                    sp.dma_start(pe_in[:, b], pe_cols[r, :]).then_inc(x_in[b], 16)

            def evacuate(eng, copy, i, which):
                eng.wait_ge(turned, i + 1)
                cols = slice(i * P, (i + 1) * P)
                four = lambda bank: ps[:, bank].rearrange("p (h t) -> p h t", h=4)
                nope, rope, bank = (qnT, qrT, 0) if which == 0 else (knT, krT, 3)
                copy(nope[:, 0:4, cols], four(bank))
                copy(nope[:, 4:8, cols], four(bank + 1))
                copy(rope[:, :, cols], four(bank + 2)).then_inc(copied, 1)

            @block.scalar
            def _(act):
                act.wait_ge(ang_ready, 1)
                nc.scalar.activation(ang[:], ang[:], ACT.Sin).then_inc(sin_done, 1)
                for i in range(TT):
                    b = i % 2
                    act.wait_ge(x_in[b], 48 * (i // 2 + 1))
                    if i >= 1:
                        act.wait_ge(sums_ready, i)
                    nc.scalar.activation(sq[:, :, 0:QK], q[:, b], ACT.Square)
                    nc.scalar.activation(sq[:, :, QK:], kn[:, b], ACT.Square)
                    nc.scalar.activation(sp_[:], pe_in[:, b], ACT.Square, accum_out=st[:, i, 3, 0:1]).then_inc(sq_done, 1)
                    act.wait_ge(sums_ready, i + 1)
                    nc.scalar.activation(st[:, i, 1], st[:, i, 0], ACT.Sqrt, scale=1.0 / QK, bias=core.eps[:]) \
                        .then_inc(rooted, 1)
                    evacuate(act, nc.scalar.copy, i, 0)
                act.wait_ge(copied, 2 * TT)

            @block.tensor
            def _(pe):
                for i in range(TT):
                    if i >= 1:
                        pe.wait_ge(copied, 2 * i)
                    pe.wait_ge(nope_ready, i + 1)
                    for z in range(2):
                        for h in range(H):
                            nc.tensor.transpose(ps[:, 3 * z + h // 4, (h % 4) * P:(h % 4 + 1) * P], qk[:, z * H + h, 0:NOPE],
                                                core.ident[:])
                    pe.wait_ge(rope_ready, i + 1)
                    for z in range(2):
                        for c in range(H // 2):
                            last = nc.tensor.transpose(ps[:, 3 * z + 2, c * P:(c + 1) * P],
                                                       ro[:, z * H + 2 * c:z * H + 2 * c + 2, :].rearrange("p h d -> p (h d)"),
                                                       core.ident[:])
                    last.then_inc(turned, 1)

            @block.gpsimd
            def _(pool):
                for i in range(TT):
                    pool.wait_ge(nope_ready, i + 1)
                    if i >= 1:
                        pool.wait_ge(rope_ready, i)
                    if i == 0:
                        pool.wait_ge(sin_done, 1)
                    half = ROPE // 2
                    s = ang[:, 0, i].unsqueeze(1).broadcast_to([P, 2 * H, half])
                    nc.gpsimd.tensor_tensor(t1[:, :, 0:half], qk[:, :, NOPE + half:], s, ALU.mult)
                    nc.gpsimd.tensor_tensor(t1[:, :, half:], qk[:, :, NOPE:NOPE + half], s, ALU.mult).then_inc(pools, 1)

            @block.vector
            def _(dve):
                ch = Chain(dve, own)
                V = nc.vector
                half = ROPE // 2
                dve.wait_ge(small_in, 64)
                ch.link(V.tensor_copy(pos[:], posi[:]))
                for i in range(TT):
                    ch.mark(V.tensor_scalar(ang[:, 0, i], inv[:], pos[:, i:i + 1], None, ALU.mult))
                ch.settle()
                ch.link(V.tensor_scalar(tmp[:], ang[:, 0], 1.0 / TWO_PI, None, ALU.mult))
                ch.link(V.tensor_scalar(tmp[:], tmp[:], MAGIC, None, ALU.add))
                ch.link(V.tensor_scalar(tmp[:], tmp[:], MAGIC, None, ALU.subtract))
                for part in (C1, C2, C3):
                    ch.link(V.scalar_tensor_tensor(ang[:, 0], tmp[:], -part, ang[:, 0], ALU.mult, ALU.add))
                ch.link(V.tensor_scalar(ang[:, 1], ang[:, 0], TWO_PI / 4, None, ALU.add))
                ch.link(V.tensor_scalar(tmp[:], ang[:, 1], TWO_PI / 2, -TWO_PI, ALU.is_gt, ALU.mult))
                ch.link(V.tensor_tensor(ang[:, 1], ang[:, 1], tmp[:], ALU.add))
                V.tensor_scalar(ang[:], ang[:], PI_DOWN, -PI_DOWN, ALU.min, ALU.max).then_inc(ang_ready, 1)
                for i in range(TT):
                    b = i % 2
                    dve.wait_ge(sq_done, i + 1)
                    ch.mark(V.reduce_sum(st[:, i, 0, 0:H], sq[:, :, 0:QK], AX_X))
                    ch.link(V.reduce_sum(st[:, i, 2, 0:H], sq[:, :, QK:], AX_X))
                    V.tensor_scalar(st[:, i, 0, H:], st[:, i, 2, 0:H], st[:, i, 3, 0:1], None, ALU.add) \
                        .then_inc(sums_ready, 1)
                    dve.wait_ge(rooted, i + 1)
                    ch.link(V.reciprocal(st[:, i, 2], st[:, i, 1]))
                    if i >= 1:
                        dve.wait_ge(turned, i)
                    rq = st[:, i, 2, 0:H].unsqueeze(2)
                    rk = st[:, i, 2, H:].unsqueeze(2)
                    ch.mark(V.tensor_tensor(qk[:, 0:H], q[:, b], rq.broadcast_to([P, H, QK]), ALU.mult))
                    ch.mark(V.tensor_tensor(qk[:, H:, 0:NOPE], kn[:, b], rk.broadcast_to([P, H, NOPE]), ALU.mult))
                    ch.mark(V.tensor_tensor(qk[:, H:, NOPE:], pe_in[:, b].unsqueeze(1).broadcast_to([P, H, ROPE]),
                                            rk.broadcast_to([P, H, ROPE]), ALU.mult))
                    ch.settle()
                    V.tensor_tensor(qk[:, 0:H], qk[:, 0:H], gq[:].unsqueeze(1).broadcast_to([P, H, QK]), ALU.mult)
                    ch.mark(V.tensor_tensor(qk[:, H:], qk[:, H:], gk[:].unsqueeze(1).broadcast_to([P, H, QK]), ALU.mult))
                    ch.settle()
                    dve.wait_ge(sin_done, 1)
                    c = ang[:, 1, i].unsqueeze(1).broadcast_to([P, 2 * H, half])
                    V.tensor_tensor(ro[:, :, 0:half], qk[:, :, NOPE:NOPE + half], c, ALU.mult).then_inc(nope_ready, 1)
                    ch.link(V.tensor_tensor(ro[:, :, half:], qk[:, :, NOPE + half:], c, ALU.mult))
                    dve.wait_ge(nope_ready, i + 1)
                    dve.wait_ge(pools, i + 1)
                    V.tensor_tensor(ro[:, :, 0:half], ro[:, :, 0:half], t1[:, :, 0:half], ALU.subtract)
                    V.tensor_tensor(ro[:, :, half:], ro[:, :, half:], t1[:, :, half:], ALU.add).then_inc(rope_ready, 1)
                    evacuate(dve, V.tensor_copy, i, 1)
                dve.wait_ge(copied, 2 * TT)


def mla_attention(core, name, qnT, knT, qrT, krT, v, o_rows):
    nc = core.nc
    SCALE = QK ** -0.5
    H = MLA_H
    units = [(qt, h) for qt in range(TT) for h in range(H)]
    groups = [(n, range(c, min(c + 4, units[n][0] + 1))) for n in range(len(units)) for c in range(0, units[n][0] + 1, 4)]
    first_group = [next(g for g, (m, _) in enumerate(groups) if m == n) for n in range(len(units))] + [len(groups)]
    copies = lambda g, which: len([x for x in range(g) if x % 2 == which])
    sem = lambda n: core.sem(f"{name}_{n}")
    s_done, masked, e_done = sem("scores_done"), sem("masked"), sem("exp_done")
    turned, own = sem("turned"), sem("dve")
    nb_ready = sem("bias_ready")
    copied = [sem("copied_act"), sem("copied_dve")]
    o_done, o_read = sem("o_done"), sem("o_read")
    barred = sem("barred")
    stored = [sem(f"stored{b}") for b in range(2)]
    with ExitStack() as ctx:
        sb = lambda n, s, d=F32: ctx.enter_context(nc.sbuf_tensor(f"{name}_{n}", s, d))
        p = sb("p", [P, 2, T])
        pT = sb("pT", [P, 2, TT, P])
        st = sb("st", [P, 2, 2])
        ls = sb("ls", [P, 2, H])
        bar = sb("bar", [P, P])
        o = sb("o", [P, 2, H, MLA_V])
        ps = ctx.enter_context(nc.psum_tensor(f"{name}_ps", [P, 2, 2 * BANK], F32))
        ps_t = ctx.enter_context(nc.psum_tensor(f"{name}_ps_t", [P, 2, BANK], F32))
        ps_o = ctx.enter_context(nc.psum_tensor(f"{name}_ps_o", [P, H, MLA_V], F32))
        with nc.Block() as block:

            @block.tensor
            def _(pe):
                def scores(n):
                    qt, h = units[n]
                    keys = (qt + 1) * P
                    r = slice(64 * (h % 2), 64 * (h % 2) + 64)
                    q = slice(qt * P, (qt + 1) * P)
                    if n >= 2:
                        pe.wait_ge(e_done, n - 1)
                    for k0 in range(0, keys, BANK):
                        k1 = min(keys, k0 + BANK)
                        nc.tensor.matmul(ps[:, n % 2, k0:k1], qnT[:, h, q], knT[:, h, k0:k1], start=True, stop=False)
                        last = nc.tensor.matmul(ps[:, n % 2, k0:k1], qrT[r, h // 2, q], krT[r, h // 2, k0:k1],
                                                start=False, stop=True)
                    last.then_inc(s_done, 1)

                def weigh(n):
                    qt, h = units[n]
                    pe.wait_ge(e_done, n + 1)
                    mine = range(first_group[n], first_group[n + 1])
                    for g in mine:
                        if g >= 2:
                            pe.wait_ge(copied[g % 2], copies(g - 1, g % 2))
                        for j, c in enumerate(groups[g][1]):
                            last = nc.tensor.transpose(ps_t[:, g % 2, j * P:(j + 1) * P], p[:, n % 2, c * P:(c + 1) * P],
                                                       core.ident[:])
                        last.then_inc(turned, 1)
                    if h % 4 == 0 and qt >= 1:
                        pe.wait_ge(o_read, 2 * (qt - 1) + h // 4 + 1)
                    for g in mine:
                        pe.wait_ge(copied[g % 2], copies(g + 1, g % 2))
                        for c in groups[g][1]:
                            last = nc.tensor.matmul(ps_o[:, h, :], pT[:, n % 2, c, :], v[:, c, h * MLA_V:(h + 1) * MLA_V],
                                                    start=(c == 0), stop=(c == qt))
                    last.then_inc(o_done, 1)

                for n in range(len(units) + 1):
                    if n < len(units):
                        scores(n)
                    if n >= 1:
                        weigh(n - 1)

            def copy_turned(eng, copy, which, n):
                for g in range(first_group[n], first_group[n + 1]):
                    if g % 2 == which:
                        eng.wait_ge(turned, g + 1)
                        if n >= 2:
                            eng.wait_ge(o_done, n - 1)
                        kt = groups[g][1]
                        copy(pT[:, n % 2, kt[0]:kt[-1] + 1, :].rearrange("p c t -> p (c t)"), ps_t[:, g % 2, 0:len(kt) * P]) \
                            .then_inc(copied[which], 1)

            @block.scalar
            def _(act):
                for n in range(len(units) + 1):
                    if n < len(units):
                        qt, h = units[n]
                        act.wait_ge(nb_ready, n + 1)
                        if n >= 2:
                            act.wait_ge(turned, first_group[n - 1])
                        if h == 0 and qt >= 2:
                            act.wait_ge(o_read, 2 * (qt - 1))
                        nc.scalar.activation(p[:, n % 2, 0:(qt + 1) * P], ps[:, n % 2, 0:(qt + 1) * P], ACT.Exp,
                                             bias=st[:, n % 2, 1:2], scale=SCALE, accum_out=ls[:, qt % 2, h:h + 1]) \
                            .then_inc(e_done, 1)
                    if n >= 1:
                        copy_turned(act, nc.scalar.copy, 0, n - 1)

            @block.vector
            def _(dve):
                ch = Chain(dve, own)
                V = nc.vector
                V.tensor_scalar(bar[:], core.causal[:], 1.0, 3.0e38, ALU.subtract, ALU.mult).then_inc(barred, 1)
                dve.wait_ge(barred, 1)
                for n in range(len(units) + 1):
                    if n < len(units):
                        qt, h = units[n]
                        dve.wait_ge(s_done, n + 1)
                        diag = ps[:, n % 2, qt * P:(qt + 1) * P]
                        ch.link(V.tensor_tensor(diag, diag, bar[:], ALU.add))
                        ch.link(V.reduce_max(st[:, n % 2, 0:1], ps[:, n % 2, 0:(qt + 1) * P], AX_X))
                        V.tensor_scalar(st[:, n % 2, 1:2], st[:, n % 2, 0:1], -SCALE, None, ALU.mult).then_inc(nb_ready, 1)
                    if n >= 1:
                        copy_turned(dve, V.tensor_copy, 1, n - 1)
                        qt, h = units[n - 1]
                        if h % 4 == 3:
                            part = slice(h - 3, h + 1)
                            dve.wait_ge(o_done, n)
                            if h == 3 and qt >= 2:
                                dve.wait_ge(stored[qt % 2], 16 * (qt // 2))
                            ch.link(V.reciprocal(ls[:, qt % 2, part], ls[:, qt % 2, part]))
                            V.tensor_tensor(o[:, qt % 2, part], ps_o[:, part],
                                            ls[:, qt % 2, part].unsqueeze(2).broadcast_to([P, 4, MLA_V]), ALU.mult) \
                                .then_inc(o_read, 1)

            @block.sync
            def _(sp):
                for qt in range(TT):
                    sp.wait_ge(o_read, 2 * qt + 2)
                    sp.dma_start(o_rows[qt * P:(qt + 1) * P, :], o[:, qt % 2].rearrange("p h d -> p (h d)")) \
                        .then_inc(stored[qt % 2], 16)
                for b in range(2):
                    sp.wait_ge(stored[b], 16 * TT // 2)


def merge(core, name, aT, bT, gT, mT):
    nc = core.nc
    BUF = 4
    loaded = [core.sem(f"{name}_loaded{b}") for b in range(BUF)]
    gated = core.sem(f"{name}_gated")
    own = core.sem(f"{name}_dve")
    pools = core.sem(f"{name}_pool")
    added = core.sem(f"{name}_added")
    high_done = core.sem(f"{name}_high_done")
    merged = core.sem(f"{name}_merged")
    with ExitStack() as ctx:
        t = ctx.enter_context(nc.sbuf_tensor(f"{name}_t", [P, BUF, 4, T], F32))
        with nc.Block() as block:

            @block.sync
            def _(sp):
                for c in range(KD):
                    if c >= BUF:
                        sp.wait_ge(merged, c - BUF + 1)
                    r = slice(c * P, (c + 1) * P)
                    for j, src in enumerate((aT[r], bT[r], gT[r], gT[D + c * P:D + (c + 1) * P])):
                        sp.dma_start(t[:, c % BUF, j], src).then_inc(loaded[c % BUF], 16)

            @block.scalar
            def _(act):
                for c in range(KD + 1):
                    if c < KD:
                        act.wait_ge(loaded[c % BUF], 64 * (c // BUF + 1))
                        nc.scalar.activation(t[:, c % BUF, 2:4], t[:, c % BUF, 2:4], ACT.Sigmoid).then_inc(gated, 1)
                    if c >= 1:
                        act.wait_ge(added, c)
                        nc.scalar.copy(mT[0][:, c - 1], t[:, (c - 1) % BUF, 0]).then_inc(high_done, 1)
                act.wait_ge(high_done, KD)

            @block.gpsimd
            def _(pool):
                for c in range(KD):
                    pool.wait_ge(gated, c + 1)
                    nc.gpsimd.tensor_tensor(t[:, c % BUF, 1], t[:, c % BUF, 1], t[:, c % BUF, 3], ALU.mult).then_inc(pools, 1)

            @block.vector
            def _(dve):
                ch = Chain(dve, own)
                for c in range(KD + 1):
                    if c < KD:
                        dve.wait_ge(gated, c + 1)
                        ch.link(nc.vector.tensor_tensor(t[:, c % BUF, 0], t[:, c % BUF, 0], t[:, c % BUF, 2], ALU.mult))
                        dve.wait_ge(pools, c + 1)
                        nc.vector.tensor_tensor(t[:, c % BUF, 0], t[:, c % BUF, 0], t[:, c % BUF, 1], ALU.add) \
                            .then_inc(added, 1)
                    if c >= 1:
                        dve.wait_ge(high_done, c)
                        low_part(nc, mT[1][:, c - 1], t[:, (c - 1) % BUF, 0], mT[0][:, c - 1]).then_inc(merged, 1)
                dve.wait_ge(merged, KD)


def load_rows(core, name, rows, dst):
    nc = core.nc
    loaded = core.sem(f"{name}_loaded")
    with nc.Block() as block:

        @block.sync
        def _(sp):
            sp.dma_start(dst, rows.rearrange("(t p) n -> p t n", p=P)).then_inc(loaded, 16)
            sp.wait_ge(loaded, 16)


def mixer2(core, inp, x3, s, x4):
    nc = core.nc
    v, at = core.v2, core.at2
    w = inp["w_in_2"][0]
    LO = 2 * D
    Q, KV = 256, 256
    HI = LO + Q + KV + ROPE
    with ExitStack() as ctx:
        uT = pair(core, ctx, "u1T", [P, KD, T])
        tiles = [(x3[i * P:(i + 1) * P, :], v[:, at["norm1_g"]], None) for i in range(TT)]
        norm_transpose(core, "norm1b", tiles, uT)
        linear(core, "in_xy", uT, KD, T, w[:, 0:LO], s["xyT"], True, 4)
        linear(core, "in_c", uT, KD, T, w[:, LO:HI], s["c_rows"], False, 2, S=288)
        linear(core, "in_g", uT, KD, T, w[:, HI:HI + 2 * D], s["gT"], True, 4)
    core.end_stage()
    with ExitStack() as ctx:
        hg = ctx.enter_context(nc.sbuf_tensor("hg", [P, KD, T], F32))
        recurrent_branch(core, inp, s["xyT"], hg)
        linear(core, "rnn_o", hg, KD, T, inp["w_rnn_o_2"][0], s["aT"], True, 4, S=256)
    core.end_stage()
    with ExitStack() as ctx:
        cT = pair(core, ctx, "cqT", [P, 2, T])
        for nm, lo, g, wt, out, slabs, width in (("q", 0, "q_norm_g", "w_uq_2", "q_rows", 4, 384),
                                                 ("kv", Q, "kv_norm_g", "w_ukv_2", "kv_rows", 4, 512)):
            tiles = [(s["c_rows"][i * P:(i + 1) * P, lo:lo + Q], v[:, at[g]], None) for i in range(TT)]
            norm_transpose(core, f"norm_{nm}", tiles, cT, width=Q)
            linear(core, f"up_{nm}", cT, 2, T, inp[wt][0], s[out], False, slabs, S=width)
    core.end_stage()
    with ExitStack() as ctx:
        sb = lambda n, sh: ctx.enter_context(nc.sbuf_tensor(n, sh, F32))
        qnT, knT = sb("qnT", [P, MLA_H, T]), sb("knT", [P, MLA_H, T])
        qrT, krT = sb("qrT", [P, MLA_H // 2, T]), sb("krT", [P, MLA_H // 2, T])
        mla_heads(core, inp, s["q_rows"], s["kv_rows"], s["c_rows"][:, Q + KV:Q + KV + ROPE], qnT, knT, qrT, krT)
        vt = sb("vt", [P, TT, MLA_H * MLA_V])
        for_heads = s["kv_rows"].rearrange("t (h x d) -> t h x d", h=MLA_H, x=2)[:, :, 1, :]
        vload = core.sem("v_loaded")
        with nc.Block() as block:

            @block.sync
            def _(sp):
                for i in range(TT):
                    sp.dma_start(vt[:, i].rearrange("p (h d) -> p h d", h=MLA_H), for_heads[i * P:(i + 1) * P]) \
                        .then_inc(vload, 16)
                sp.wait_ge(vload, 16 * TT)

        mla_attention(core, "mla", qnT, knT, qrT, krT, vt, s["o_rows"])
    core.end_stage()
    with ExitStack() as ctx:
        oT = pair(core, ctx, "mla_oT", [P, KD, T])
        turn_rows(core, "oturn", s["o_rows"], oT, KD)
        linear(core, "mla_o", oT, KD, T, inp["w_mla_o_2"][0], s["bT"], True, 2)
    core.end_stage()
    with ExitStack() as ctx:
        mT = pair(core, ctx, "mergedT", [P, KD, T])
        merge(core, "merge", s["aT"], s["bT"], s["gT"], mT)
        residual_product(core, "out2", mT, inp["w_out_2"][0], x3, None, x4)
    core.end_stage()


def ffn2(core, inp, x4, xn, y, out):
    nc = core.nc
    g = core.v2[:, core.at2["norm2_g"]]
    with ExitStack() as ctx:
        core.ctx_keep = lambda n, s, d: ctx.enter_context(nc.sbuf_tensor(n, s, d))
        rt = Routing(core, "rt2", inp["exp_w1_2"].shape[1])
        with ExitStack() as c2:
            h2T = c2.enter_context(nc.sbuf_tensor("h4T", [P, KD, T], F32))
            tiles = [(x4[i * P:(i + 1) * P, :], g, None) for i in range(TT)]
            norm_transpose(core, "norm2b", tiles, h2T, xn)
            route(core, "route2", h2T, inp["router_wg_2"][0], inp["router_we_2"][0],
                  inp["router_bg_2"][0], inp["router_be_2"][0], rt, y)
        weights = [inp[n][0] for n in ("exp_w1_2", "exp_w3_2", "exp_w2_2")]
        experts(core, "exp2", rt, xn, g, None, *weights, y)
        experts_beyond(core, "over2", rt, xn, g, None, *weights, y)
        combine(core, "comb2", rt, y, x4, None, out)


def vector_tables2(core, inp):
    rows = lambda a: a.rearrange("(n p) -> n p", p=P)
    core.v2, core.at2 = column_vectors(core, "v2", [
        ("norm1_g", rows(inp["norm1_g_2"][0])), ("norm2_g", rows(inp["norm2_g_2"][0])),
        ("conv_w", inp["conv_w_2"][0].rearrange("j (n p) -> (j n) p", p=P)), ("conv_b", rows(inp["conv_b_2"][0])),
        ("lru_ba", rows(inp["lru_ba_2"][0])), ("lru_bx", rows(inp["lru_bx_2"][0])),
        ("lru_lambda", rows(inp["lru_lambda_2"][0])), ("q_norm_g", rows(inp["q_norm_g_2"][0])),
        ("kv_norm_g", rows(inp["kv_norm_g_2"][0]))])


def inv_freq():
    return (10000.0 ** (-np.arange(0, ROPE, 2) / ROPE)).astype(np.float32)


WEIGHTS = ["x", "c", "ctx", "c_ctx", "w_ada", "b_ada", "norm_mix_g", "norm_ffn_g", "w_in", "da_lambda", "da_subln_g",
           "gla_gate_w2", "gla_gate_b", "gla_norm_g", "w_out", "router_group_w", "router_group_b", "router_expert_w",
           "router_expert_b", "expert_w_gate", "expert_w_up", "expert_w_down", "final_norm_g", "positions_2",
           "norm1_g_2", "w_in_2", "conv_w_2", "conv_b_2", "lru_wa_2", "lru_ba_2", "lru_wx_2", "lru_bx_2",
           "lru_lambda_2", "w_rnn_o_2", "q_norm_g_2", "w_uq_2", "kv_norm_g_2", "w_ukv_2", "qk_norm_q_g_2",
           "qk_norm_k_g_2", "w_mla_o_2", "w_out_2", "norm2_g_2", "router_wg_2", "router_bg_2", "router_we_2",
           "router_be_2", "exp_w1_2", "exp_w3_2", "exp_w2_2"]


def program(nc, inp, out):
    n_ctx = inp["ctx"].shape[1]

    def scratch(name, shape):
        return nc.dram_tensor(f"scratch_{name}", shape, F32).ap()

    with ExitStack() as ctx:
        core = Core(nc, ctx)
        build_constants(core, inp)
        vector_tables(core, inp)
        vector_tables2(core, inp)
        modulation(core, inp)
        core.end_stage()
        proj = scratch("proj", (n_ctx + T, inp["w_in"].shape[2]))
        mix = scratch("mix", (T, D))
        in_projection(core, inp, proj)
        diff_attention(core, inp, proj, mix)
        core.end_stage()
        gated_linear_attention(core, inp, proj, mix)
        core.end_stage()
        x1, x2, x3, x4 = (scratch(f"x{i}", (T, D)) for i in range(1, 5))
        xn1, xn2 = scratch("xn1", (T, D)), scratch("xn2", (T, D))
        y1 = scratch("y1", ((N_EXPERTS1 + OVER) * SLOTS, D))
        y2 = scratch("y2", ((N_EXPERTS2 + OVER) * SLOTS, D))
        ffn1(core, inp, mix, x1, xn1, y1, x2)
        row_norm(core, "final", x2, inp["final_norm_g"], x3)
        core.end_stage()
        s = {name: scratch(name, shape) for name, shape in (
            ("xyT", (2 * D, T)), ("c_rows", (T, 576)), ("gT", (2 * D, T)), ("aT", (D, T)), ("bT", (D, T)),
            ("q_rows", (T, MLA_H * QK)), ("kv_rows", (T, MLA_H * (NOPE + MLA_V))), ("o_rows", (T, MLA_H * MLA_V)))}
        mixer2(core, inp, x3, s, x4)
        ffn2(core, inp, x4, xn2, y2, out[0])


N_EXPERTS1, N_EXPERTS2 = 32, 64


def kernel(**inputs):
    import concourse.bacc as bacc
    from concourse.bass_utils import run_bass_kernel_spmd

    nc = bacc.Bacc("TRN2", target_bir_lowering=False, num_devices=1)
    cos, sin = rope_tables()
    given = {name: np.ascontiguousarray(inputs[name]) for name in WEIGHTS}
    given.update(rope_cos=cos, rope_sin=sin, inv_freq=inv_freq())
    arrays, aps = {}, {}
    for name, a in given.items():
        arrays[f"in_{name}"] = a
        aps[name] = nc.dram_tensor(f"in_{name}", a.shape, mybir.dt.from_np(a.dtype), kind="ExternalInput").ap()
    out = nc.dram_tensor("out_0", (1, T, D), F32, kind="ExternalOutput").ap()
    program(nc, aps, out)
    r = run_bass_kernel_spmd(nc, [arrays], core_ids=[0])
    return r.results[0]["out_0"]
```
